# Optimizing a Trainium2 kernel written in Bass

```python
import jax, jax.numpy as jnp
from jax import lax
import numpy as np

D_MODEL = 1024
BATCH = 1
SEQ = 256
DEPTH = 2
DEC_BATCH = 8
DEC_SEQ = 1
PAST_LEN = 2048
PAGE_SIZE = 128

D_CONV = D_MODEL // 2
D_POOL = D_MODEL - D_CONV
CONV_W = 3
POOL_WINDOWS = (2, 4, 8, 16)
N_POOL_GROUPS = len(POOL_WINDOWS)
POOL_GROUP = D_POOL // N_POOL_GROUPS
POOL_MAX = max(POOL_WINDOWS)
D_IN = 3 * D_CONV + D_POOL
PEER_HEADS = 8
N_KEYS = 128
N_EXPERTS = N_KEYS * N_KEYS
PEER_TOPK = 16
D_KEY = 256
D_HALF = D_KEY // 2
PEER_BLOCK = 256
ALPHA = (2 * DEPTH) ** 0.25
BETA = (8 * DEPTH) ** -0.25
LN_EPS = 1e-5

kernel_name = 'hymba_conv_pool_peer_decoder_step'

def _ln_stats(x):
    xf = x.astype(jnp.float32)
    mu = jnp.mean(xf, axis=-1, keepdims=True)
    var = jnp.mean(jnp.square(xf - mu), axis=-1, keepdims=True)
    return (xf - mu) * lax.rsqrt(var + LN_EPS)

def layer_norm(x, g, b):
    return (_ln_stats(x) * g + b).astype(x.dtype)

def modulate(x, shift, scale):
    return (_ln_stats(x) * (1.0 + scale[:, None, :]) + shift[:, None, :]).astype(x.dtype)

def short_conv_group(bg, cg, hc, prefix, conv_w):
    T = hc.shape[1]
    u = cg * hc
    u_ext = jnp.concatenate([prefix.astype(u.dtype), u], axis=1)
    y = u_ext[:, 0:T] * conv_w[0]
    for k in range(1, CONV_W):
        y = y + u_ext[:, k:k + T] * conv_w[k]
    return bg * y, u_ext[:, -(CONV_W - 1):]

def pool_group(hp, prefix, start_pos, pool_w, pool_scale):
    Bsz, T, _ = hp.shape
    P = POOL_MAX - 1
    p_ext = jnp.concatenate([prefix.astype(hp.dtype), hp], axis=1)
    cs = jnp.cumsum(p_ext.astype(jnp.float32), axis=1)
    cs = jnp.pad(cs, ((0, 0), (1, 0), (0, 0)))
    pos = jnp.arange(T, dtype=jnp.float32) + start_pos
    hpf = hp.astype(jnp.float32)
    outs = []
    for g, w in enumerate(POOL_WINDOWS):
        sl = slice(g * POOL_GROUP, (g + 1) * POOL_GROUP)
        win_sum = cs[:, P + 1:P + 1 + T, sl] - cs[:, P + 1 - w:P + 1 - w + T, sl]
        cnt = jnp.minimum(pos + 1.0, float(w))[None, :, None]
        outs.append(win_sum / cnt - hpf[:, :, sl])
    pooled = jnp.stack(outs, axis=2).astype(hp.dtype)
    mixed = jnp.einsum('btgc,gcd->btgd', pooled, pool_w).reshape(Bsz, T, D_POOL)
    return mixed * pool_scale, p_ext[:, -P:]

def peer_ffn(h, w_q, sub_keys, u_tab, v_tab):
    Bsz, T, D = h.shape
    flat = h.reshape(Bsz * T, D)
    n = flat.shape[0]
    pad = (-n) % PEER_BLOCK
    blocks = jnp.pad(flat, ((0, pad), (0, 0))).reshape(-1, PEER_BLOCK, D)

    def one_block(hb):
        q = (hb @ w_q).reshape(PEER_BLOCK, PEER_HEADS, 2, D_HALF)
        s = jnp.einsum('thpc,hpkc->thpk', q, sub_keys).astype(jnp.float32)
        s1, i1 = lax.top_k(s[:, :, 0], PEER_TOPK)
        s2, i2 = lax.top_k(s[:, :, 1], PEER_TOPK)
        cand = (s1[..., :, None] + s2[..., None, :]).reshape(PEER_BLOCK, PEER_HEADS, PEER_TOPK * PEER_TOPK)
        top_s, top_i = lax.top_k(cand, PEER_TOPK)
        e1 = jnp.take_along_axis(i1, top_i // PEER_TOPK, axis=-1)
        e2 = jnp.take_along_axis(i2, top_i % PEER_TOPK, axis=-1)
        experts = e1 * N_KEYS + e2
        gates = jax.nn.softmax(top_s, axis=-1)
        u = u_tab[experts]
        act = jnp.einsum('thkd,td->thk', u, hb).astype(jnp.float32)
        coef = (gates * jax.nn.gelu(act, approximate=False)).astype(hb.dtype)
        return jnp.einsum('thk,thkd->td', coef, v_tab[experts])

    out = lax.map(one_block, blocks).reshape(-1, D)[:n]
    return out.reshape(Bsz, T, D)

def run_group(x, c, conv_prefix, pool_prefix, start_pos,
              w_ada, b_ada, w_in, conv_w, pool_w, pool_scale, w_out, ln1_g, ln1_b,
              w_q, sub_keys, u_experts, v_experts, ln2_g, ln2_b):
    conv_states, pool_states = [], []
    for l in range(DEPTH):
        mod = jax.nn.silu(c) @ w_ada[l] + b_ada[l]
        sh1, sc1, g1, sh2, sc2, g2 = jnp.split(mod, 6, axis=-1)
        h = modulate(x, sh1, sc1)
        z = h @ w_in[l]
        bg, cg, hc, hp = jnp.split(z, [D_CONV, 2 * D_CONV, 3 * D_CONV], axis=-1)
        conv_out, conv_st = short_conv_group(bg, cg, hc, conv_prefix[l], conv_w[l])
        pool_out, pool_st = pool_group(hp, pool_prefix[l], start_pos, pool_w[l], pool_scale[l])
        mix = jnp.concatenate([conv_out, pool_out], axis=-1) @ w_out[l]
        x = layer_norm(ALPHA * x + g1[:, None, :] * mix, ln1_g[l], ln1_b[l])
        h2 = modulate(x, sh2, sc2)
        f = peer_ffn(h2, w_q[l], sub_keys[l], u_experts[l], v_experts[l])
        x = layer_norm(ALPHA * x + g2[:, None, :] * f, ln2_g[l], ln2_b[l])
        conv_states.append(conv_st)
        pool_states.append(pool_st)
    return x, jnp.stack(conv_states), jnp.stack(pool_states)

def setup_inputs(seed: int = 0) -> dict:
    key = jax.random.key(seed)
    ks = jax.random.split(key, 24)
    nrm = jax.random.normal
    f32 = jnp.float32
    D = D_MODEL
    return {
        'x_prompt': nrm(ks[0], (BATCH, SEQ, D), f32),
        'x_sample': nrm(ks[1], (DEC_BATCH, DEC_SEQ, D), f32),
        'state_conv': nrm(ks[2], (DEPTH, DEC_BATCH, CONV_W - 1, D_CONV), f32),
        'state_pool': nrm(ks[3], (DEPTH, DEC_BATCH, POOL_MAX - 1, D_POOL), f32),
        'c_prompt': nrm(ks[4], (BATCH, D), f32),
        'c_sample': nrm(ks[5], (DEC_BATCH, D), f32),
        'w_ada': nrm(ks[6], (DEPTH, D, 6 * D), f32) * (0.5 * D ** -0.5),
        'b_ada': nrm(ks[7], (DEPTH, 6 * D), f32) * 0.02,
        'w_in': nrm(ks[8], (DEPTH, D, D_IN), f32) * D ** -0.5,
        'conv_w': nrm(ks[9], (DEPTH, CONV_W, D_CONV), f32) * CONV_W ** -0.5,
        'pool_w': nrm(ks[10], (DEPTH, N_POOL_GROUPS, POOL_GROUP, POOL_GROUP), f32) * POOL_GROUP ** -0.5,
        'pool_scale': 1.0 + 0.1 * nrm(ks[11], (DEPTH, D_POOL), f32),
        'w_out': nrm(ks[12], (DEPTH, D, D), f32) * (BETA * D ** -0.5),
        'ln1_g': 1.0 + 0.02 * nrm(ks[13], (DEPTH, D), f32),
        'ln1_b': 0.02 * nrm(ks[14], (DEPTH, D), f32),
        'w_q': nrm(ks[15], (DEPTH, D, PEER_HEADS * D_KEY), f32) * D ** -0.5,
        'sub_keys': nrm(ks[16], (DEPTH, PEER_HEADS, 2, N_KEYS, D_HALF), f32) * D_HALF ** -0.5,
        'u_experts': nrm(ks[17], (DEPTH, N_EXPERTS, D), f32) * D ** -0.5,
        'v_experts': nrm(ks[18], (DEPTH, N_EXPERTS, D), f32) * BETA,
        'ln2_g': 1.0 + 0.02 * nrm(ks[19], (DEPTH, D), f32),
        'ln2_b': 0.02 * nrm(ks[20], (DEPTH, D), f32),
    }

def reference(x_prompt, x_sample, state_conv, state_pool, c_prompt, c_sample,
              w_ada, b_ada, w_in, conv_w, pool_w, pool_scale, w_out, ln1_g, ln1_b,
              w_q, sub_keys, u_experts, v_experts, ln2_g, ln2_b):
    weights = (w_ada, b_ada, w_in, conv_w, pool_w, pool_scale, w_out, ln1_g, ln1_b,
               w_q, sub_keys, u_experts, v_experts, ln2_g, ln2_b)
    n_prompt = x_prompt.shape[0]
    zero_conv = jnp.zeros((DEPTH, n_prompt, CONV_W - 1, D_CONV), x_prompt.dtype)
    zero_pool = jnp.zeros((DEPTH, n_prompt, POOL_MAX - 1, D_POOL), x_prompt.dtype)
    y_prompt, conv_prompt, pool_prompt = run_group(
        x_prompt, c_prompt, zero_conv, zero_pool, 0, *weights)
    y_sample, conv_sample, pool_sample = run_group(
        x_sample, c_sample, state_conv, state_pool, PAST_LEN, *weights)
    return (y_prompt, y_sample, conv_prompt, pool_prompt, conv_sample, pool_sample)


_drawn_inputs = setup_inputs


def setup_inputs(seed=0):
    import zlib

    import numpy as np

    out = dict(_drawn_inputs(seed))
    spreads = {}
    factors = {'pool_scale': 4.023}
    for name, (base, spread) in spreads.items():
        noise = np.random.default_rng([zlib.crc32(name.encode()), seed]).standard_normal(out[name].shape)
        drawn = base * np.exp(spread * noise) if base else spread * noise
        out[name] = __import__('jax').numpy.asarray(drawn.astype(out[name].dtype))
    for name, factor in factors.items():
        out[name] = (out[name] * factor).astype(out[name].dtype)
    return out
```

```python
import numpy as np
import concourse.bass as bass
from concourse import mybir
from contextlib import ExitStack

F32 = mybir.dt.float32
U32 = mybir.dt.uint32
ALU = mybir.AluOpType
ACT = mybir.ActivationFunctionType
AX = mybir.AxisListType

D = 1024
DEPTH = 2
SEQ = 256
NS = 8
CONV_W = 3
WINDOWS = (2, 4, 8, 16)
HIST = max(WINDOWS) - 1
HEADS = 8
N_KEYS = 128
N_EXPERTS = N_KEYS * N_KEYS
TOPK = 16
ALPHA = float((2 * DEPTH) ** 0.25)
EPS = 1e-5

P = 128
DC = D // P
CB = D // 2 // P
ZB = 4 * CB
HP = 2 * HEADS
NC9 = 1 + NS
NMAX = P + NS
BW = 256
BK = DC * BW
WSLOTS = 3
KPC = 4
RC = 3
SLOT = 2 * D
TILE_CHUNKS = HEADS * TOPK // KPC
SAMPLE_CHUNKS = HEADS * NS * TOPK // P // KPC
SH1, SC1, G1, SH2, SC2, G2 = (i * DC for i in range(6))
MINUS = -3.0e38

B_ADA = 0
CONV = B_ADA + DEPTH * 6 * DC
PSC = CONV + DEPTH * CB * CONV_W
COND = PSC + DEPTH * CB
SMALL = COND + DC * NC9
O_CP = 0
O_PP = O_CP + CB * 2
O_CS = O_PP + CB * HIST
O_PS = O_CS + CB * NS * 2
ST_OUT = O_PS + CB * NS * HIST

FRONTS = 2 * DEPTH


def stage_chunks(s):
    return TILE_CHUNKS + (SAMPLE_CHUNKS if s % 2 else 0)


def first_chunk(s):
    return sum(stage_chunks(i) for i in range(s))


def weight_blocks():
    order = [("ada", 0, i) for i in range(6 * D // BW)]

    def front(f):
        return ([("in", f, i) for i in range(2 * D // BW)] + [("pool", f, 0)] + [("out", f, i) for i in range(D // BW)]
                + [("ln1", f, 0)] + [("q", f, i) for i in range(2 * D // BW)] + [("keys", f, 0)])
    order += front(0)
    for s in range(FRONTS):
        if s + 1 < FRONTS:
            order += front(s + 1)
        if s == 0:
            order += [("ada", 1, i) for i in range(6 * D // BW)]
        order += [("ln2", s, 0)]
    return order


PLAN = {
    0: [(5, "project"), (11, "mix"), (17, "query"), (20, "pick_keys"), (23, "pick_experts"),
        (26, "decode"), (29, "sample_pick"), (31, "ada")],
    1: [(5, "project"), (11, "mix"), (17, "query"), (20, "pick_keys"), (23, "pick_experts"),
        (26, "decode")],
    2: [(5, "project"), (11, "mix"), (17, "query"), (20, "pick_keys"), (23, "pick_experts"),
        (26, "decode"), (29, "sample_pick")],
    3: [],
}
FRONT_STEPS = ["project", "mix", "query", "pick_keys", "pick_experts", "decode", "sample_pick"]


def build_trunk(nc, x, xs, small, w_ada, w_in, w_out, w_q, keys, pool_w, ln1, ln2, conv_st, pool_st, uv,
                y, ys, st_new, bounce):
    BLOCKS = weight_blocks()
    AT = {b: n for n, b in enumerate(BLOCKS)}

    ctx = ExitStack()
    with ctx:
        def sb(name, shape, dt=F32):
            return ctx.enter_context(nc.sbuf_tensor(name, shape, dt))

        def sem(name):
            return ctx.enter_context(nc.semaphore(name))

        ring = sb("ring", [P, RC * KPC, SLOT])
        wring = sb("wring", [P, WSLOTS, BK])
        X = [sb(f"X{g}", [P, D]) for g in range(2)]
        Xs = sb("Xs", [NS, D])
        h2 = [sb(f"h2_{g}", [P, D]) for g in range(2)]
        h2rep = sb("h2rep", [P, D])
        hT = sb("hT", [P, DC, NMAX])
        zT = sb("zT", [P, ZB, NMAX])
        catT = sb("catT", [P, DC, NMAX])
        big0 = sb("big0", [P, HEADS * TOPK * TOPK])
        big1 = sb("big1", [P, HEADS * TOPK * TOPK])
        uext = sb("uext", [P, CB, 2 + P])
        pext = sb("pext", [P, CB, HIST + P])
        cs = sb("cs", [P, CB, NS, CONV_W])
        ps = sb("ps", [P, CB, NS, HIST + 1])
        sts = sb("sts", [P, ST_OUT])
        mod = [sb(f"mod{l}", [P, 6 * DC, NC9]) for l in range(DEPTH)]
        sm = sb("sm", [P, SMALL])
        csil = sb("csil", [P, DC, NC9])
        diag = sb("diag", [P, RC, KPC, P])
        act_in = sb("act_in", [P, RC, KPC])
        act_out = sb("act_out", [P, RC, KPC])
        ixs = sb("ixs", [P, RC, KPC], U32)
        idx = [sb(f"idx{g}", [P, HEADS * TOPK], U32) for g in range(2)]
        gates = [sb(f"gates{g}", [P, HEADS * TOPK]) for g in range(2)]
        s_pack = sb("s_pack", [P, 2, TOPK, 2], U32)
        s_ig = sb("s_ig", [P, 4, 2, 2], U32)
        kv = sb("kv", [P, HP, TOPK])
        ki = sb("ki", [P, HP, TOPK], U32)
        kf = sb("kf", [P, HP, TOPK])
        ev = sb("ev", [P, HEADS, TOPK])
        ei = sb("ei", [P, HEADS, TOPK], U32)
        ea = sb("ea", [P, HEADS, TOPK], U32)
        fa = sb("fa", [P, HEADS, TOPK])
        fb = sb("fb", [P, HEADS, TOPK])
        e1 = sb("e1", [P, HEADS * TOPK])
        e2 = sb("e2", [P, HEADS * TOPK])
        rs = sb("rs", [P, HEADS])
        hs = sb("hs", [P, DC, NS])
        bn = sb("bn", [P, 2, 6])
        mv = sb("mv", [P, 2])
        ve = sb("ve", [P, 1])
        sd = sb("sd", [P, 1])
        rstd = sb("rstd", [P, 1])
        ident = sb("ident", [P, P])
        iota = sb("iota", [P, TOPK])
        mask = sb("mask", [P, NS])
        inv = sb("inv", [P, CB, TOPK])

        tok = catT[:, :, :].rearrange("p a b -> p (a b)")[:, 0:D]
        toks = h2rep[0:NS, :]
        xns = big1[0:NS, 0:D]
        hsrep = big0[:, 0:D].rearrange("p (c t) -> p c t", c=DC)

        acc = ctx.enter_context(nc.psum_tensor("acc", [P, D], F32))
        scores = ctx.enter_context(nc.psum_tensor("scores", [P, HP, N_KEYS], F32))
        work = [ctx.enter_context(nc.psum_tensor(f"work{i}", [P, 512], F32)) for i in range(2)]

        consts_in = sem("consts_in")
        state_in = sem("state_in")
        w_landed = [sem(f"w_landed{i}") for i in range(WSLOTS)]
        w_used = [sem(f"w_used{i}") for i in range(WSLOTS)]
        made = sem("made")
        work_full = sem("work_full")
        work_free = sem("work_free")
        dve_done = sem("dve_done")
        silu_done = sem("silu_done")
        mod_raw = sem("mod_raw")
        mod_ready = sem("mod_ready")
        var_ready = sem("var_ready")
        std_ready = sem("std_ready")
        xn_ready = sem("xn_ready")
        hT_ready = sem("hT_ready")
        hs_raw = sem("hs_raw")
        hs_ready = sem("hs_ready")
        z_ready = sem("z_ready")
        pooled_ready = sem("pooled_ready")
        cat_ready = sem("cat_ready")
        mT_ready = sem("mT_ready")
        ms_ready = sem("ms_ready")
        tok_ready = sem("tok_ready")
        h2_ready = sem("h2_ready")
        rep_ready = sem("rep_ready")
        q_ready = sem("q_ready")
        scores_ready = sem("scores_ready")
        scores_free = sem("scores_free")
        exp_in = sem("exp_in")
        exp_done = sem("exp_done")
        picks_ready = sem("picks_ready")
        pack_ready = sem("pack_ready")
        pack_out = sem("pack_out")
        spread = sem("spread")
        states_made = sem("states_made")
        ix_staged = sem("ix_staged")
        gathers_go = sem("gathers_go")
        uv_landed = [sem(f"uv_landed{i}") for i in range(RC)]
        acts_ready = sem("acts_ready")
        gelu_ready = sem("gelu_ready")
        diag_ready = sem("diag_ready")
        chunk_used = sem("chunk_used")
        acc_free = sem("acc_free")
        g2_ready = sem("g2_ready")
        x_ready = sem("x_ready")
        stored = sem("stored")

        def wslot(n):
            return wring[:, n % WSLOTS, :]

        def arrived(eng, n):
            eng.wait_ge(w_landed[n % WSLOTS], 16 * (n // WSLOTS + 1))
            return wslot(n)

        def over_chunks(eng, s, lo, hi, body):
            def place(c):
                return (first_chunk(s) + c) % RC, (first_chunk(s) + c) // RC + 1

            g = lo
            while g < hi and place(g)[0]:
                body(g, *place(g))
                g += 1
            turns = (hi - g) // RC
            if turns > 1:
                with eng.Fori(0, turns) as t:
                    for r in range(RC):
                        body(t * RC + (g + r), r, t + place(g)[1])
                g += turns * RC
            while g < hi:
                body(g, *place(g))
                g += 1

        def run_stage(eng, s, first, body, last, steps, lag=0):
            over_chunks(eng, s, 0, 1, first)
            at = 1
            for after, step in PLAN[s]:
                end = max(at, min(after + 1, TILE_CHUNKS - 1) - lag)
                over_chunks(eng, s, at, end, body)
                at = end
                steps[step](s + 1)
            over_chunks(eng, s, at, TILE_CHUNKS - 1, body)
            over_chunks(eng, s, TILE_CHUNKS - 1, TILE_CHUNKS, last)

        block = ctx.enter_context(nc.Block())

        @block.sync
        def _(sp):
            sp.dma_start(sm[:, :], small).then_inc(consts_in, 16)
            sp.dma_start(X[0][:, :], x[0:P, :]).then_inc(consts_in, 16)
            sp.dma_start(X[1][:, :], x[P:2 * P, :]).then_inc(consts_in, 16)
            sp.dma_start(Xs[:, :], xs).then_inc(consts_in, 16)
            stores = 0

            def load(n):
                kind, f, i = BLOCKS[n]
                layer = f if kind == "ada" else f // 2
                src = {"ada": w_ada, "in": w_in, "out": w_out, "q": w_q}.get(kind)
                if n >= WSLOTS:
                    sp.wait_ge(w_used[n % WSLOTS], n // WSLOTS)
                dst = wslot(n)
                if src is not None:
                    src = src[layer, i]
                elif kind == "keys":
                    src = keys[layer]
                elif kind == "pool":
                    dst, src = dst[:, 0:CB * P], pool_w[layer]
                else:
                    src = (ln1 if kind == "ln1" else ln2)[layer:layer + 1, :].broadcast_to([P, 2 * D])
                sp.dma_start(dst, src).then_inc(w_landed[n % WSLOTS], 16)

            n = 0
            for f in range(FRONTS):
                layer = f // 2
                if f % 2 == 1:
                    if layer:
                        sp.wait_ge(states_made, layer)
                    sp.dma_start(cs[:, :, :, :], conv_st[layer]).then_inc(state_in, 16)
                    sp.dma_start(ps[:, :, :, :], pool_st[layer]).then_inc(state_in, 16)
                while BLOCKS[n] != ("q", f, 0):
                    load(n)
                    n += 1
                if f % 2 == 1:
                    sp.wait_ge(states_made, layer + 1)
                    sp.dma_start(st_new[layer], sts[:, :]).then_inc(stored, 16)
                    stores += 1
            while n < len(BLOCKS):
                load(n)
                n += 1
            sp.wait_ge(x_ready, 1)
            sp.dma_start(y[0:P, :], X[0][:, :]).then_inc(stored, 16)
            sp.wait_ge(x_ready, 2)
            sp.dma_start(y[P:2 * P, :], X[1][:, :]).then_inc(stored, 16)
            sp.wait_ge(x_ready, 3)
            sp.dma_start(ys, Xs[:, :]).then_inc(stored, 16)
            sp.wait_ge(stored, 16 * (stores + 3))

        @block.gpsimd
        def _(pool):
            n_made = 0

            def make(ins):
                nonlocal n_made
                n_made += 1
                ins.then_inc(made, 1)
                pool.wait_ge(made, n_made)

            make(nc.gpsimd.memset(ident[:, :], 0.0))
            make(nc.gpsimd.affine_select(out=ident[:, :], in_=ident[:, :], compare_op=ALU.not_equal, fill=1.0,
                                         base=0, pattern=[[-1, P]], channel_multiplier=1))
            make(nc.gpsimd.iota(iota[:, :], [[1, TOPK]], base=0, channel_multiplier=0,
                                allow_small_or_imprecise_dtypes=True))
            make(nc.gpsimd.memset(mask[:, :], 1.0))
            make(nc.gpsimd.affine_select(out=mask[:, :], in_=mask[:, :], compare_op=ALU.is_ge, fill=0.0,
                                         base=0, pattern=[[-TOPK, NS]], channel_multiplier=1))
            make(nc.gpsimd.affine_select(out=mask[:, :], in_=mask[:, :], compare_op=ALU.is_ge, fill=0.0,
                                         base=TOPK - 1, pattern=[[TOPK, NS]], channel_multiplier=-1))
            for b, w in enumerate(WINDOWS):
                make(nc.gpsimd.memset(inv[:, b, :], 1.0 / w))
            for t in range(HIST):
                b = min(b for b, w in enumerate(WINDOWS) if w > t + 1)
                make(nc.gpsimd.memset(inv[:, b:CB, t:t + 1], 1.0 / (t + 1)))

            def gather(s, rows):
                G0 = first_chunk(s)

                def body(c, r, n):
                    if not isinstance(c, int) or G0 + c >= RC:
                        pool.wait_ge(chunk_used, c + (G0 - RC + 1))
                    out, src = rows(c, ixs[:, r, :])
                    nc.gpsimd.tensor_copy(out, src).then_inc(ix_staged, 1)
                    pool.wait_ge(ix_staged, c + (G0 + 1))
                    pool.sem_inc(gathers_go, 1)
                    for j in range(KPC):
                        nc.gpsimd.indirect_dma_start(ring[:, r * KPC + j, :], None, uv,
                                                     bass.IndirectOffsetOnAxis(ixs[:, r, j:j + 1], 0))\
                            .then_inc(uv_landed[r], 16)
                return body

            for s in range(FRONTS):
                pool.wait_ge(picks_ready, s + 1)
                body = gather(s, lambda c, to, g=s % 2: (to, idx[g][:, bass.ds(c * KPC, KPC)]))
                over_chunks(pool, s, 0, RC, body)
                over_chunks(pool, s, RC, TILE_CHUNKS, body)
                if s % 2:
                    pool.wait_ge(spread, 16 * (s // 2 + 1))
                    for c in range(TILE_CHUNKS, TILE_CHUNKS + SAMPLE_CHUNKS):
                        q = (c - TILE_CHUNKS) * KPC // 2
                        body = gather(s, lambda c, to, q=q: (to.rearrange("p (q g) -> p q g", g=2),
                                                             s_ig[:, q:q + KPC // 2, 0, :]))
                        over_chunks(pool, s, c, c + 1, body)

        @block.scalar
        def _(act):
            item = [0]

            def drain(*copies):
                act.wait_ge(work_full, item[0] + 1)
                bank = work[item[0] % 2]
                for out, pick, scale, bias in copies[:-1]:
                    nc.scalar.activation(out, pick(bank), ACT.Identity, bias=bias, scale=scale)
                out, pick, scale, bias = copies[-1]
                last = nc.scalar.activation(out, pick(bank), ACT.Identity, bias=bias, scale=scale)
                last.then_inc(work_free, 1)
                item[0] += 1
                return item[0]

            def after_drain(sig):
                act.wait_ge(work_free, item[0])
                act.sem_inc(sig, 1)

            def cols(lo, hi, parts=P):
                return lambda bank: bank[0:parts, lo:hi]

            def root(parts=P, n=[0]):
                n[0] += 1
                act.wait_ge(var_ready, n[0])
                nc.scalar.activation(sd[0:parts, :], ve[0:parts, :], ACT.Sqrt).then_inc(std_ready, 1)

            def transposed(m, shift, scale, with_samples):
                for half in range(2):
                    drain(*[(hT[:, half * 4 + c, 0:P], cols(c * P, (c + 1) * P),
                             m[:, scale + half * 4 + c, 0:1], m[:, shift + half * 4 + c, 0:1])
                            for c in range(4)])
                after_drain(hT_ready)
                if with_samples:
                    drain((hs[:, :, :].rearrange("p a b -> p (a b)"), cols(0, DC * NS), 1.0, 0.0))
                    after_drain(hs_raw)

            def project(f):
                m, smp = mod[f // 2], f % 2
                n = P + NS * smp
                root()
                if smp:
                    root(NS)
                transposed(m, SH1, SC1, smp)
                for c in range(ZB):
                    drain((zT[:, c, 0:n], cols(0, n), 1.0, 0.0))
                after_drain(z_ready)

            def mix(f):
                l, m, smp = f // 2, mod[f // 2], f % 2
                n = P + NS * smp
                for g in range(CB):
                    drain((catT[:, CB + g, 0:n], cols(0, n), sm[:, PSC + l * CB + g:PSC + l * CB + g + 1], 0.0))
                after_drain(cat_ready)
                for c in range(DC):
                    copies = [(hT[:, c, 0:P], cols(0, P), m[:, G1 + c, 0:1], 0.0)]
                    if smp:
                        copies.append((hT[:, c, P:NMAX], cols(P, NMAX), 1.0, 0.0))
                    drain(*copies)
                after_drain(mT_ready)

            def query(f):
                m, smp = mod[f // 2], f % 2
                n = P + NS * smp
                for half in range(2):
                    drain((tok[:, half * 512:(half + 1) * 512], cols(0, 512), 1.0, 0.0))
                if smp:
                    for half in range(2):
                        drain((toks[:, half * 512:(half + 1) * 512], cols(0, 512, NS), 1.0, 0.0))
                after_drain(tok_ready)
                root()
                root()
                if smp:
                    root(NS)
                    root(NS)
                transposed(m, SH2, SC2, smp)
                for half in range(2):
                    drain((h2[f % 2][:, half * 512:(half + 1) * 512], cols(0, 512), 1.0, 0.0))
                if smp:
                    for half in range(2):
                        drain((h2rep[:, half * 512:(half + 1) * 512], cols(0, 512), 1.0, 0.0))
                after_drain(h2_ready)
                for c in range(HP):
                    drain((zT[:, c, 0:n], cols(0, n), 1.0, 0.0))
                after_drain(q_ready)

            n_exp = [0]

            def exps(nh):
                n_exp[0] += 1
                act.wait_ge(exp_in, n_exp[0])
                nc.scalar.activation(kv[:, 0:nh, :], kv[:, 0:nh, :], ACT.Exp).then_inc(exp_done, 1)

            def decode(f):
                exps(HEADS)

            def sample_pick(f):
                if f % 2 == 0:
                    return
                exps(2)
                act.wait_ge(pack_ready, f // 2 + 1)
                for q in range(4):
                    act.dma_start(bounce[q].rearrange("a t x -> t a x"),
                                  s_pack[32 * q:32 * q + NS, :, :, :].rearrange("p a k g -> p a (k g)"))\
                        .then_inc(pack_out, 16)
                act.wait_ge(pack_out, 64 * (f // 2 + 1))
                act.dma_start(s_ig[:, :, :, :].rearrange("p q a g -> p (q a) g"),
                              bounce.rearrange("q a t (k g) -> (t k) (q a) g", g=2)).then_inc(spread, 16)

            def ada(layer):
                for i in range(6 * D // BW):
                    drain((mod[layer][:, 2 * i:2 * i + 2, :].rearrange("p a b -> p (a b)"), cols(0, 2 * NC9), 1.0, 0.0))
                after_drain(mod_raw)

            steps = {"project": project, "mix": mix, "query": query, "pick_keys": lambda f: None,
                     "pick_experts": lambda f: None, "decode": decode, "sample_pick": sample_pick,
                     "ada": lambda f: ada(1)}

            def gelu(s):
                G0 = first_chunk(s)

                def body(c, r, n):
                    act.wait_ge(acts_ready, c + (G0 + 1))
                    nc.scalar.activation(act_out[:, r, :], act_in[:, r, :], ACT.Gelu).then_inc(gelu_ready, 1)
                return body

            def gate2(f, parts):
                out = tok if parts == P else toks
                for half in range(2):
                    drain((out[:, half * 512:(half + 1) * 512], cols(0, 512, parts), 1.0, 0.0))
                after_drain(g2_ready)
                root(parts)

            act.wait_ge(consts_in, 16 * 4)
            nc.scalar.activation(csil[:, :, :].rearrange("p a b -> p (a b)"), sm[:, COND:SMALL],
                                 ACT.Silu).then_inc(silu_done, 1)
            ada(0)
            act.wait_ge(mod_ready, 1)
            for step in FRONT_STEPS:
                steps[step](0)
            for s in range(FRONTS):
                body = gelu(s)
                run_stage(act, s, body, body, body, steps)
                if s % 2:
                    for c in range(TILE_CHUNKS, TILE_CHUNKS + SAMPLE_CHUNKS):
                        if c == TILE_CHUNKS + 1:
                            gate2(s, P)
                        over_chunks(act, s, c, c + 1, body)
                    gate2(s, NS)
                else:
                    gate2(s, P)

        @block.vector
        def _(dve):
            counts = {}

            def link(ins, sig=dve_done):
                counts[id(sig)] = counts.get(id(sig), 0) + 1
                ins.then_inc(sig, 1)
                dve.wait_ge(sig, counts[id(sig)])

            roots = [0]

            def normalise(src, out, parts=P, sig=dve_done):
                for i in range(2):
                    last = nc.vector.bn_stats(bn[0:parts, i, :], src[:, i * 512:(i + 1) * 512])
                link(last)
                link(nc.vector.bn_aggr(mv[0:parts, :], bn[0:parts, :, :].rearrange("p a b -> p (a b)")))
                nc.vector.tensor_scalar(ve[0:parts, :], mv[0:parts, 1:2], EPS, None, ALU.add).then_inc(var_ready, 1)
                roots[0] += 1
                dve.wait_ge(std_ready, roots[0])
                link(nc.vector.reciprocal(rstd[0:parts, :], sd[0:parts, :]))
                link(nc.vector.tensor_scalar(out, src, mv[0:parts, 0:1], rstd[0:parts, 0:1], ALU.subtract, ALU.mult),
                     sig)

            def gain(t, n, parts=P, sig=dve_done, inc=1):
                gb = arrived(dve, n)
                link(nc.vector.tensor_tensor(t, t, gb[0:parts, 0:D], ALU.mult))
                return nc.vector.tensor_tensor(t, t, gb[0:parts, D:2 * D], ALU.add)

            def modulate_samples(f, shift, scale):
                m = mod[f // 2]
                link(nc.vector.tensor_tensor(hs[:, :, :], hs[:, :, :], m[:, scale:scale + DC, 1:NC9], ALU.mult))
                link(nc.vector.tensor_tensor(hT[:, :, P:NMAX], hs[:, :, :], m[:, shift:shift + DC, 1:NC9], ALU.add),
                     hs_ready)

            def project(f):
                smp = f % 2
                normalise(X[f % 2][:, :], h2[f % 2][:, :], P, xn_ready)
                if smp:
                    normalise(Xs[:, :], xns, NS, xn_ready)
                    dve.wait_ge(hs_raw, f // 2 * 2 + 1)
                    modulate_samples(f, SH1, SC1)

            def conv_weight(l, b, k):
                at = CONV + (l * CB + b) * CONV_W + k
                return sm[:, at:at + 1]

            def mix(f):
                l, smp = f // 2, f % 2
                if f % 2 == 0:
                    nc.vector.memset(uext[:, :, 0:2], 0.0)
                    link(nc.vector.memset(pext[:, :, 0:HIST], 0.0))
                else:
                    nc.vector.tensor_copy(uext[:, :, 0:2], uext[:, :, P:P + 2])
                    link(nc.vector.tensor_copy(pext[:, :, 0:HIST], pext[:, :, P:P + HIST]))
                dve.wait_ge(z_ready, f + 1)
                nc.vector.tensor_tensor(uext[:, :, 2:2 + P], zT[:, CB:2 * CB, 0:P], zT[:, 2 * CB:3 * CB, 0:P], ALU.mult)
                link(nc.vector.tensor_copy(pext[:, :, HIST:HIST + P], zT[:, 3 * CB:ZB, 0:P]))
                yT = big0[:, 0:CB * P].rearrange("p (b t) -> p b t", b=CB)
                s0 = big1[:, 0:CB * (HIST + P)].rearrange("p (b t) -> p b t", b=CB)
                s1 = big0[:, CB * P:CB * P + CB * (HIST + P)].rearrange("p (b t) -> p b t", b=CB)
                E = HIST + P
                for b in range(CB):
                    nc.vector.tensor_scalar(yT[:, b, :], uext[:, b, 0:P], conv_weight(l, b, 0), None, ALU.mult)
                link(nc.vector.tensor_tensor(s0[:, :, 1:E], pext[:, :, 1:E], pext[:, :, 0:E - 1], ALU.add))
                for b in range(CB):
                    nc.vector.scalar_tensor_tensor(yT[:, b, :], uext[:, b, 1:1 + P], conv_weight(l, b, 1),
                                                   yT[:, b, :], ALU.mult, ALU.add)
                link(nc.vector.tensor_tensor(s1[:, 1:CB, 3:E], s0[:, 1:CB, 3:E], s0[:, 1:CB, 1:E - 2], ALU.add))
                for b in range(CB):
                    nc.vector.scalar_tensor_tensor(yT[:, b, :], uext[:, b, 2:2 + P], conv_weight(l, b, 2),
                                                   yT[:, b, :], ALU.mult, ALU.add)
                link(nc.vector.tensor_tensor(s0[:, 2:CB, 7:E], s1[:, 2:CB, 7:E], s1[:, 2:CB, 3:E - 4], ALU.add))
                nc.vector.tensor_tensor(catT[:, 0:CB, 0:P], zT[:, 0:CB, 0:P], yT, ALU.mult)
                link(nc.vector.tensor_tensor(s1[:, 3:CB, HIST:E], s0[:, 3:CB, HIST:E], s0[:, 3:CB, 7:E - 8], ALU.add))
                for b, w in enumerate(WINDOWS):
                    last = nc.vector.scalar_tensor_tensor(zT[:, 3 * CB + b, 0:P], (s0, s1)[b % 2][:, b, HIST:E], 1.0 / w,
                                                          pext[:, b, HIST:E], ALU.mult, ALU.subtract)
                if f % 2 == 0:
                    link(last)
                    for b in range(CB):
                        last = nc.vector.tensor_tensor(zT[:, 3 * CB + b, 0:TOPK], (s0, s1)[b % 2][:, b, HIST:HIST + TOPK],
                                                       inv[:, b, :], ALU.mult)
                    link(last)
                    last = nc.vector.tensor_tensor(zT[:, 3 * CB:ZB, 0:TOPK], zT[:, 3 * CB:ZB, 0:TOPK],
                                                   pext[:, :, HIST:HIST + TOPK], ALU.subtract)
                if smp:
                    link(last)
                    dve.wait_ge(state_in, 32 * (l + 1))
                    nc.vector.tensor_tensor(cs[:, :, :, 2:3].rearrange("p b t o -> p b (t o)"),
                                            zT[:, CB:2 * CB, P:NMAX], zT[:, 2 * CB:3 * CB, P:NMAX], ALU.mult)
                    link(nc.vector.tensor_copy(ps[:, :, :, HIST:HIST + 1].rearrange("p b t o -> p b (t o)"),
                                               zT[:, 3 * CB:ZB, P:NMAX]))
                    ysT = big0[:, 0:CB * NS].rearrange("p (b t) -> p b t", b=CB)
                    sw = big0[:, CB * NS:2 * CB * NS].rearrange("p (b t) -> p b t", b=CB)
                    for b, w in enumerate(WINDOWS):
                        nc.vector.tensor_scalar(ysT[:, b, :], cs[:, b, :, 0], conv_weight(l, b, 0), None, ALU.mult)
                        last = nc.vector.tensor_reduce(sw[:, b, :], ps[:, b, :, HIST + 1 - w:HIST + 1], AX.X, ALU.add)
                    link(last)
                    for k in (1, 2):
                        for b in range(CB):
                            last = nc.vector.scalar_tensor_tensor(ysT[:, b, :], cs[:, b, :, k], conv_weight(l, b, k),
                                                                  ysT[:, b, :], ALU.mult, ALU.add)
                        link(last)
                    for b, w in enumerate(WINDOWS):
                        nc.vector.scalar_tensor_tensor(zT[:, 3 * CB + b, P:NMAX], sw[:, b, :], 1.0 / w, ps[:, b, :, HIST],
                                                       ALU.mult, ALU.subtract)
                    last = nc.vector.tensor_tensor(catT[:, 0:CB, P:NMAX], zT[:, 0:CB, P:NMAX], ysT, ALU.mult)
                link(last, pooled_ready)
                if smp:
                    if l:
                        dve.wait_ge(stored, 16 * l)
                    nc.vector.tensor_copy(sts[:, O_CP:O_PP].rearrange("p (b k) -> p b k", b=CB), uext[:, :, P:P + 2])
                    nc.vector.tensor_copy(sts[:, O_PP:O_CS].rearrange("p (b k) -> p b k", b=CB), pext[:, :, P:P + HIST])
                    nc.vector.tensor_copy(sts[:, O_CS:O_PS].rearrange("p (b t k) -> p (b t) k", b=CB, t=NS),
                                          cs[:, :, :, 1:3].rearrange("p b t k -> p (b t) k"))
                    nc.vector.tensor_copy(sts[:, O_PS:ST_OUT].rearrange("p (b t k) -> p (b t) k", b=CB, t=NS),
                                          ps[:, :, :, 1:HIST + 1].rearrange("p b t k -> p (b t) k"))\
                        .then_inc(states_made, 1)
                    dve.wait_ge(mT_ready, f + 1)
                    link(nc.vector.tensor_tensor(hT[:, :, P:NMAX], hT[:, :, P:NMAX], mod[l][:, G1:G1 + DC, 1:NC9],
                                                 ALU.mult), ms_ready)

            def query(f):
                l, smp = f // 2, f % 2
                xt = X[f % 2][:, :]
                dve.wait_ge(tok_ready, f + 1)
                link(nc.vector.scalar_tensor_tensor(xt, xt, ALPHA, tok, ALU.mult, ALU.add))
                normalise(xt, xt)
                n = AT["ln1", f, 0]
                last = gain(xt, n)
                if not smp:
                    last.then_inc(w_used[n % WSLOTS], 1)
                    dve.wait_ge(w_used[n % WSLOTS], n // WSLOTS + 1)
                else:
                    link(last)
                normalise(xt, h2[f % 2][:, :], P, xn_ready)
                if smp:
                    xt = Xs[:, :]
                    link(nc.vector.scalar_tensor_tensor(xt, xt, ALPHA, toks, ALU.mult, ALU.add))
                    normalise(xt, xt, NS)
                    last = gain(xt, n, NS)
                    last.then_inc(w_used[n % WSLOTS], 1)
                    dve.wait_ge(w_used[n % WSLOTS], n // WSLOTS + 1)
                    normalise(xt, xns, NS, xn_ready)
                    dve.wait_ge(hs_raw, f // 2 * 2 + 2)
                    modulate_samples(f, SH2, SC2)
                    for c in range(DC):
                        last = nc.vector.tensor_copy(hsrep[:, c, :].rearrange("p (t k) -> p t k", k=TOPK),
                                                     hT[:, c, P:NMAX].unsqueeze(2).broadcast_to([P, NS, TOPK]))
                    link(last, rep_ready)

            def search(src, tmp, values, places, free=None):
                n = src.shape[1]
                for i in range(n):
                    last = nc.vector.max(values[:, i, 0:8], src[:, i, :])
                link(last)
                for i in range(n):
                    nc.vector.max_index(places[:, i, 0:8], values[:, i, 0:8], src[:, i, :])
                    last = nc.vector.match_replace(tmp[:, i, :], values[:, i, 0:8], src[:, i, :], MINUS)
                link(last, free or dve_done)
                for i in range(n):
                    last = nc.vector.max(values[:, i, 8:16], tmp[:, i, :])
                link(last)
                for i in range(n):
                    last = nc.vector.max_index(places[:, i, 8:16], values[:, i, 8:16], tmp[:, i, :])
                link(last)

            n_scores = [0]

            def pick_keys(f, nh=HEADS):
                n_scores[0] += 1
                dve.wait_ge(scores_ready, n_scores[0])
                tmp = big0[:, 0:2 * nh * N_KEYS].rearrange("p (i k) -> p i k", k=N_KEYS)
                search(scores[:, 0:2 * nh, :], tmp, kv, ki, scores_free)

            def pick_experts(f, nh=HEADS):
                nc.vector.tensor_copy(kf[:, 0:2 * nh, :], ki[:, 0:2 * nh, :])
                pairs = big1[:, 0:nh * 256].rearrange("p (h i j) -> p h i j", h=nh, i=TOPK)
                v4 = kv[:, 0:2 * nh, :].rearrange("p (h s) k -> p h s k", s=2)
                one = v4[:, :, 0, :].unsqueeze(3).broadcast_to([P, nh, TOPK, TOPK])
                two = v4[:, :, 1, :].unsqueeze(2).broadcast_to([P, nh, TOPK, TOPK])
                link(nc.vector.tensor_tensor(pairs, one, two, ALU.add))
                tmp = big0[:, 0:nh * 256].rearrange("p (i k) -> p i k", k=256)
                search(big1[:, 0:nh * 256].rearrange("p (i k) -> p i k", k=256), tmp, ev, ei)

            n_exp = [0]

            def decode(f, nh=HEADS, rows=None, gate=None):
                l = f // 2
                rows = idx[f % 2][:, :] if rows is None else rows
                gate = gates[f % 2][:, :].rearrange("p (h k) -> p h k", k=TOPK) if gate is None else gate
                n = nh * TOPK
                ex = kv[:, 0:nh, :]
                link(nc.vector.tensor_tensor(ex, ev[:, 0:nh, :],
                                             ev[:, 0:nh, 0:1].broadcast_to([P, nh, TOPK]), ALU.subtract), exp_in)
                link(nc.vector.tensor_scalar(ea[:, 0:nh, :], ei[:, 0:nh, :], 4, None, ALU.logical_shift_right))
                link(nc.vector.tensor_copy(fa[:, 0:nh, :], ea[:, 0:nh, :]))
                link(nc.vector.tensor_scalar(ea[:, 0:nh, :], ei[:, 0:nh, :], TOPK - 1, None, ALU.bitwise_and))
                link(nc.vector.tensor_copy(fb[:, 0:nh, :], ea[:, 0:nh, :]))
                k4 = kf[:, 0:2 * nh, :].rearrange("p (h s) k -> p h s k", s=2)
                for place, half, hit, out in ((fa, 0, big0, e1), (fb, 1, big1, e2)):
                    h3 = hit[:, 0:n * TOPK].rearrange("p (a j) -> p a j", j=TOPK)
                    h4 = hit[:, 0:n * TOPK].rearrange("p (h a j) -> p h a j", h=nh, j=TOPK)
                    flat = place[:, 0:nh, :].rearrange("p h k -> p (h k)").unsqueeze(2).broadcast_to([P, n, TOPK])
                    link(nc.vector.tensor_tensor(h3, flat, iota[:, :].unsqueeze(1).broadcast_to([P, n, TOPK]), ALU.is_equal))
                    link(nc.vector.tensor_tensor(h4, h4, k4[:, :, half, :].unsqueeze(2).broadcast_to([P, nh, TOPK, TOPK]),
                                                 ALU.mult))
                    link(nc.vector.tensor_reduce(out[:, 0:n], h3, AX.X, ALU.add))
                link(nc.vector.scalar_tensor_tensor(e1[:, 0:n], e1[:, 0:n], float(N_KEYS), e2[:, 0:n], ALU.mult, ALU.add))
                e3 = e1[:, 0:n].rearrange("p (h k) -> p h k", k=TOPK) if len(rows.shape) == 3 else e1[:, 0:n]
                nc.vector.tensor_scalar(rows, e3, float(l * N_EXPERTS), None, ALU.add)
                n_exp[0] += 1
                dve.wait_ge(exp_done, n_exp[0])
                link(nc.vector.tensor_reduce(rs[:, 0:nh], ex, AX.X, ALU.add))
                link(nc.vector.reciprocal(rs[:, 0:nh], rs[:, 0:nh]))
                link(nc.vector.tensor_tensor(gate, ex, rs[:, 0:nh].unsqueeze(2).broadcast_to([P, nh, TOPK]),
                                             ALU.mult), picks_ready if nh == HEADS else pack_ready)

            def sample_pick(f):
                if f % 2 == 0:
                    return
                pick_keys(f, 2)
                pick_experts(f, 2)
                if f // 2:
                    dve.wait_ge(pack_out, 64 * (f // 2))
                decode(f, 2, s_pack[:, 0, :, :].rearrange("p k h -> p h k"),
                       s_pack[:, 1, :, :].bitcast(F32).rearrange("p k h -> p h k"))

            def ada(layer):
                dve.wait_ge(mod_raw, layer + 1)
                m = mod[layer]
                b = sm[:, B_ADA + layer * 6 * DC:B_ADA + (layer + 1) * 6 * DC]
                link(nc.vector.tensor_tensor(m[:, :, :], m[:, :, :], b.unsqueeze(2).broadcast_to([P, 6 * DC, NC9]), ALU.add))
                nc.vector.tensor_scalar(m[:, SC1:SC1 + DC, :], m[:, SC1:SC1 + DC, :], 1.0, None, ALU.add)
                link(nc.vector.tensor_scalar(m[:, SC2:SC2 + DC, :], m[:, SC2:SC2 + DC, :], 1.0, None, ALU.add), mod_ready)

            steps = {"project": project, "mix": mix, "query": query, "pick_keys": pick_keys,
                     "pick_experts": pick_experts, "decode": decode, "sample_pick": sample_pick,
                     "ada": lambda f: ada(1)}

            def chunk_work(s, gate_of, xt, base, width):
                G0 = first_chunk(s)

                def dots(c, r, n):
                    dve.wait_ge(uv_landed[r], n * (16 * KPC))
                    for j in range(KPC):
                        u = ring[:, r * KPC + j, 0:D]
                        last = nc.vector.scalar_tensor_tensor(u, u, 1.0, xt, ALU.mult, ALU.mult,
                                                              accum_out=act_in[:, r, j:j + 1])
                    last.then_inc(acts_ready, 1)

                def diags(c, r, n=None):
                    dve.wait_ge(gelu_ready, c + (G0 + 1))
                    for j in range(KPC):
                        last = nc.vector.tensor_scalar(diag[:, r, j, 0:width], base[:, 0:width], act_out[:, r, j:j + 1],
                                                       gate_of(c, j), ALU.mult, ALU.mult)
                    last.then_inc(diag_ready, 1)

                def both(c, r, n):
                    dots(c, r, n)
                    diags(c - 1, (r - 1) % RC)

                return dots, diags, both

            gate2s = [0]
            xr = [0]

            def finish(s, parts):
                t = tok if parts == P else toks
                xt = X[s % 2][:, :] if parts == P else Xs[:, :]
                n = AT["ln2", s, 0]
                gate2s[0] += 1
                dve.wait_ge(g2_ready, gate2s[0])
                done = first_chunk(s) + (TILE_CHUNKS if parts == P else stage_chunks(s))
                dve.wait_ge(chunk_used, done)
                link(nc.vector.tensor_tensor(t, t, acc[0:parts, :], ALU.mult), acc_free)
                link(nc.vector.scalar_tensor_tensor(xt, xt, ALPHA, t, ALU.mult, ALU.add))
                normalise(xt, xt, parts)
                last = gain(xt, n, parts)
                if s >= FRONTS - 2:
                    link(last, x_ready)
                    last = None
                if parts == NS or s % 2 == 0:
                    if last is None:
                        last = nc.vector.tensor_copy(ve[0:1, :], mv[0:1, 0:1])
                    last.then_inc(w_used[n % WSLOTS], 1)
                    dve.wait_ge(w_used[n % WSLOTS], n // WSLOTS + 1)
                elif last is not None:
                    link(last)

            dve.wait_ge(made, 6 + len(WINDOWS) + HIST)
            dve.wait_ge(consts_in, 16 * 4)
            ada(0)
            for step in FRONT_STEPS:
                steps[step](0)
            for s in range(FRONTS):
                g = s % 2

                def tile_gate(c, j, g=g):
                    return gates[g][:, bass.ds(c * KPC + j, 1)]

                dots, diags, both = chunk_work(s, tile_gate, h2[g][:, :], ident, P)
                run_stage(dve, s, dots, both, both, steps)
                last_c = TILE_CHUNKS - 1
                diags(last_c, (first_chunk(s) + last_c) % RC)
                if s % 2:
                    def sample_gate(c, j):
                        at = (c - TILE_CHUNKS) * KPC + j
                        return s_ig[:, at // 2, 1, at % 2:at % 2 + 1].bitcast(F32)

                    dve.wait_ge(spread, 16 * (s // 2 + 1))
                    dots, diags, both = chunk_work(s, sample_gate, h2rep[:, :], mask, NS)
                    over_chunks(dve, s, TILE_CHUNKS, TILE_CHUNKS + 1, dots)
                    finish(s, P)
                    diags(TILE_CHUNKS, (first_chunk(s) + TILE_CHUNKS) % RC)
                    c = TILE_CHUNKS + 1
                    over_chunks(dve, s, c, c + 1, dots)
                    diags(c, (first_chunk(s) + c) % RC)
                    finish(s, NS)
                else:
                    finish(s, P)

        @block.tensor
        def _(pe):
            item = [0]

            def bank():
                if item[0] >= 2:
                    pe.wait_ge(work_free, item[0] - 1)
                b = work[item[0] % 2]
                item[0] += 1
                return b

            def transposes(src, parts=P):
                for half in range(2):
                    b = bank()
                    for c in range(4):
                        last = nc.tensor.transpose(b[:, c * P:(c + 1) * P], src[:, (half * 4 + c) * P:(half * 4 + c + 1) * P],
                                                   ident[:, :])
                    last.then_inc(work_full, 1)

            def to_channels(f, nth):
                smp = f % 2
                n_xn = [0, 2, 6, 8][f] + (nth * 2 if smp else nth)
                pe.wait_ge(xn_ready, n_xn + 1)
                transposes(h2[f % 2])
                if smp:
                    pe.wait_ge(xn_ready, n_xn + 2)
                    b = bank()
                    for c in range(DC):
                        last = nc.tensor.matmul(b[:, c * NS:(c + 1) * NS], xns[:, c * P:(c + 1) * P], ident[0:NS, 0:NS],
                                                start=True, stop=True)
                    last.then_inc(work_full, 1)
                pe.wait_ge(hT_ready, 2 * f + nth + 1)
                if smp:
                    pe.wait_ge(hs_ready, f // 2 * 2 + nth + 1)

            def to_tokens(f):
                for half in range(2):
                    b = bank()
                    for c in range(4):
                        last = nc.tensor.transpose(b[:, c * P:(c + 1) * P], hT[:, half * 4 + c, 0:P], ident[:, :])
                    last.then_inc(work_full, 1)

            def dense(kind, f, blocks, rhs, n):
                for i in range(blocks):
                    nb = AT[kind, f, i]
                    w = arrived(pe, nb).rearrange("p (k c) -> p k c", k=DC)
                    for j in range(BW // P):
                        b = bank()
                        for k in range(DC):
                            last = nc.tensor.matmul(b[:, 0:n], w[:, k, j * P:(j + 1) * P], rhs[:, k, 0:n],
                                                    start=(k == 0), stop=(k == DC - 1))
                        last.then_inc(work_full, 1)
                    pe.wait_ge(work_full, item[0])
                    pe.sem_inc(w_used[nb % WSLOTS], 1)

            def project(f):
                to_channels(f, 0)
                dense("in", f, 2 * D // BW, hT, P + NS * (f % 2))

            def mix(f):
                n = P + NS * (f % 2)
                pe.wait_ge(pooled_ready, f + 1)
                nb = AT["pool", f, 0]
                w = arrived(pe, nb)
                for g in range(CB):
                    b = bank()
                    nc.tensor.matmul(b[:, 0:n], w[:, g * P:(g + 1) * P], zT[:, 3 * CB + g, 0:n], start=True, stop=True)\
                        .then_inc(work_full, 1)
                pe.wait_ge(work_full, item[0])
                pe.sem_inc(w_used[nb % WSLOTS], 1)
                pe.wait_ge(cat_ready, f + 1)
                dense("out", f, D // BW, catT, n)

            def query(f):
                smp = f % 2
                pe.wait_ge(mT_ready, f + 1)
                to_tokens(f)
                if smp:
                    pe.wait_ge(ms_ready, f // 2 + 1)
                    for half in range(2):
                        b = bank()
                        for c in range(4):
                            last = nc.tensor.matmul(b[0:NS, c * P:(c + 1) * P], hT[:, half * 4 + c, P:NMAX], ident[:, :],
                                                    start=True, stop=True)
                        last.then_inc(work_full, 1)
                to_channels(f, 1)
                to_tokens(f)
                if smp:
                    pe.wait_ge(rep_ready, f // 2 + 1)
                    for half in range(2):
                        b = bank()
                        for c in range(4):
                            last = nc.tensor.matmul(b[:, c * P:(c + 1) * P], hsrep[:, half * 4 + c, :], ident[:, :], start=True, stop=True)
                        last.then_inc(work_full, 1)
                dense("q", f, 2 * D // BW, hT, P + NS * smp)

            n_scores = [0]

            def pick_keys(f):
                pe.wait_ge(q_ready, f + 1)
                if n_scores[0]:
                    pe.wait_ge(scores_free, n_scores[0])
                n_scores[0] += 1
                nb = AT["keys", f, 0]
                k = arrived(pe, nb).rearrange("p (i c) -> p i c", c=N_KEYS)
                for i in range(HP):
                    last = nc.tensor.matmul(scores[:, i, :], zT[:, i, 0:P], k[:, i, :], start=True, stop=True)
                last.then_inc(scores_ready, 1)
                if f % 2 == 0:
                    pe.wait_ge(scores_ready, n_scores[0])
                    pe.sem_inc(w_used[nb % WSLOTS], 1)

            def sample_pick(f):
                if f % 2 == 0:
                    return
                pe.wait_ge(scores_free, n_scores[0])
                n_scores[0] += 1
                nb = AT["keys", f, 0]
                k = wslot(nb).rearrange("p (i c) -> p i c", c=N_KEYS)
                for g in range(2):
                    for q in range(4):
                        for half in range(2):
                            i = 2 * (4 * g + q) + half
                            last = nc.tensor.matmul(scores[32 * q:32 * q + NS, 2 * g + half, :], zT[:, i, P:NMAX],
                                                    k[:, i, :], start=True, stop=True)
                last.then_inc(scores_ready, 1)
                pe.wait_ge(scores_ready, n_scores[0])
                pe.sem_inc(w_used[nb % WSLOTS], 1)

            def ada(layer):
                for i in range(6 * D // BW):
                    nb = AT["ada", layer, i]
                    w = arrived(pe, nb).rearrange("p (k c) -> p k c", k=DC)
                    b = bank()
                    for j in range(BW // P):
                        for k in range(DC):
                            last = nc.tensor.matmul(b[:, j * NC9:(j + 1) * NC9], w[:, k, j * P:(j + 1) * P], csil[:, k, :],
                                                    start=(k == 0), stop=(k == DC - 1))
                    last.then_inc(work_full, 1)
                    pe.wait_ge(work_full, item[0])
                    pe.sem_inc(w_used[nb % WSLOTS], 1)

            def nothing(f):
                pass

            steps = {"project": project, "mix": mix, "query": query, "pick_keys": pick_keys, "pick_experts": nothing,
                     "decode": nothing, "sample_pick": sample_pick, "ada": lambda f: ada(1)}

            def summing(s, width):
                G0 = first_chunk(s)

                def body(c, r, n, first=False, last_one=False):
                    pe.wait_ge(diag_ready, c + (G0 + 1))
                    for j in range(KPC):
                        for half in range(2):
                            last = nc.tensor.matmul(acc[0:width, half * 512:(half + 1) * 512], diag[:, r, j, 0:width],
                                                    ring[:, r * KPC + j, D + half * 512:D + (half + 1) * 512],
                                                    start=(first and j == 0), stop=(last_one and j == KPC - 1))
                    last.then_inc(chunk_used, 1)
                return body

            def gate2(s, parts):
                m = mod[s // 2]
                for half in range(2):
                    b = bank()
                    for c in range(4):
                        col = m[:, G2 + half * 4 + c, 0:1].broadcast_to([P, P]) if parts == P else m[:, G2 + half * 4 + c, 1:NC9]
                        last = nc.tensor.matmul(b[0:parts, c * P:(c + 1) * P], col, ident[:, :], start=True, stop=True)
                    last.then_inc(work_full, 1)

            pe.wait_ge(made, 2)
            pe.wait_ge(consts_in, 16 * 4)
            pe.wait_ge(silu_done, 1)
            ada(0)
            for step in FRONT_STEPS:
                steps[step](0)
            accs = [0]
            for s in range(FRONTS):
                body = summing(s, P)
                if accs[0]:
                    pe.wait_ge(acc_free, accs[0])
                run_stage(pe, s, lambda c, r, n: body(c, r, n, first=True), body,
                          lambda c, r, n: body(c, r, n, last_one=True), steps, lag=1)
                accs[0] += 1
                gate2(s, P)
                if s % 2:
                    body = summing(s, NS)
                    pe.wait_ge(acc_free, accs[0])
                    for c in range(SAMPLE_CHUNKS):
                        g = TILE_CHUNKS + c
                        over_chunks(pe, s, g, g + 1, lambda *at, c=c: body(*at, first=(c == 0),
                                                                           last_one=(c == SAMPLE_CHUNKS - 1)))
                    accs[0] += 1
                    gate2(s, NS)


def kernel(x_prompt, x_sample, state_conv, state_pool, c_prompt, c_sample, w_ada, b_ada, w_in, conv_w, pool_w,
           pool_scale, w_out, ln1_g, ln1_b, w_q, sub_keys, u_experts, v_experts, ln2_g, ln2_b):
    import concourse.bacc as _bacc
    from concourse.bass_utils import run_bass_kernel_spmd as _run

    a = {k: np.asarray(v) for k, v in locals().items() if not k.startswith("_")}

    def blocks(w):
        n = w.shape[2] // BW
        return np.ascontiguousarray(w.reshape(DEPTH, DC, P, n, BW).transpose(0, 3, 2, 1, 4)).reshape(DEPTH, n, P, BK)

    def per_channel(v, lead):
        v = v.reshape(*lead, -1, P)
        return np.moveaxis(v, -1, 0)

    cond = per_channel(np.concatenate([a["c_prompt"], a["c_sample"]]), (NC9,))
    small = np.concatenate([
        per_channel(a["b_ada"], (DEPTH,)).reshape(P, -1),
        per_channel(a["conv_w"], (DEPTH, CONV_W)).transpose(0, 1, 3, 2).reshape(P, -1),
        per_channel(a["pool_scale"], (DEPTH,)).reshape(P, -1),
        cond.transpose(0, 2, 1).reshape(P, -1)], axis=1)

    def states(s, width):
        s = per_channel(s, s.shape[:3]).transpose(1, 0, 4, 2, 3)
        return np.ascontiguousarray(np.concatenate([s, np.zeros(s.shape[:4] + (1,), s.dtype)], axis=4))

    arrays = {
        "x": a["x_prompt"].reshape(SEQ, D), "xs": a["x_sample"].reshape(NS, D), "small": small,
        "w_ada": blocks(a["w_ada"]), "w_in": blocks(a["w_in"]), "w_out": blocks(a["w_out"]), "w_q": blocks(a["w_q"]),
        "keys": a["sub_keys"].transpose(0, 4, 1, 2, 3).reshape(DEPTH, P, HP * N_KEYS),
        "pool_w": a["pool_w"].transpose(0, 2, 1, 3).reshape(DEPTH, P, CB * P),
        "ln1": np.concatenate([a["ln1_g"], a["ln1_b"]], axis=1), "ln2": np.concatenate([a["ln2_g"], a["ln2_b"]], axis=1),
        "conv_st": states(a["state_conv"], 3), "pool_st": states(a["state_pool"], 16),
        "uv": np.concatenate([a["u_experts"].reshape(-1, D), a["v_experts"].reshape(-1, D)], axis=1),
    }
    arrays = {f"in_{k}": np.ascontiguousarray(v) for k, v in arrays.items()}
    outs = {"y": (SEQ, D), "ys": (NS, D), "st_new": (DEPTH, P, ST_OUT)}

    nc = _bacc.Bacc("TRN2", target_bir_lowering=False, num_devices=1)
    ins = [nc.dram_tensor(k, v.shape, F32, kind="ExternalInput").ap() for k, v in arrays.items()]
    out = [nc.dram_tensor(f"out_{k}", v, F32, kind="ExternalOutput").ap() for k, v in outs.items()]
    bounce = nc.dram_tensor("bounce", (4, 2, NS, 2 * TOPK), U32, kind="Internal").ap()
    build_trunk(nc, *ins, *out, bounce)
    r = _run(nc, [arrays], core_ids=[0]).results[0]

    st = r["out_st_new"]

    def rows(part, *dims):
        v = part.reshape(DEPTH, P, CB, *dims)
        return np.moveaxis(v, (2, 1), (-2, -1)).reshape(DEPTH, *dims, CB * P)

    return (r["out_y"].reshape(1, SEQ, D), r["out_ys"].reshape(NS, 1, D),
            rows(st[:, :, O_CP:O_PP], 1, 2), rows(st[:, :, O_PP:O_CS], 1, HIST),
            rows(st[:, :, O_CS:O_PS], NS, 2), rows(st[:, :, O_PS:ST_OUT], NS, HIST))
```

```python
import numpy as np
import concourse.bass as bass
from concourse import mybir
from contextlib import ExitStack

F32 = mybir.dt.float32
U32 = mybir.dt.uint32
ALU = mybir.AluOpType
ACT = mybir.ActivationFunctionType
AX = mybir.AxisListType

D = 1024
DEPTH = 2
SEQ = 256
NS = 8
CONV_W = 3
WINDOWS = (2, 4, 8, 16)
HIST = max(WINDOWS) - 1
HEADS = 8
N_KEYS = 128
N_EXPERTS = N_KEYS * N_KEYS
TOPK = 16
ALPHA = float((2 * DEPTH) ** 0.25)
EPS = 1e-5

P = 128
DC = D // P
CB = D // 2 // P
ZB = 4 * CB
HP = 2 * HEADS
NC9 = 1 + NS
NMAX = P + NS
BW = 256
BK = DC * BW
WSLOTS = 4
KPC = 2
RC = 6
SLOT = 2 * D
TILE_CHUNKS = HEADS * TOPK // KPC
SAMPLE_CHUNKS = HEADS * NS * TOPK // P // KPC
PG = 2
SH1, SC1, G1, SH2, SC2, G2 = (i * DC for i in range(6))
MINUS = -3.0e38

B_ADA = 0
CONV = B_ADA + DEPTH * 6 * DC
PSC = CONV + DEPTH * CB * CONV_W
COND = PSC + DEPTH * CB
SMALL = COND + DC * NC9
O_CP = 0
O_PP = O_CP + CB * 2
O_CS = O_PP + CB * HIST
O_PS = O_CS + CB * NS * 2
ST_OUT = O_PS + CB * NS * HIST

FRONTS = 2 * DEPTH
W_STEPS = {"in": 2 * D // BW, "out": D // BW, "q": 2 * D // BW}
ADA_BLOCKS = 6 * D // BW
ADA_FIRST = 2 * D // BW


def stage_chunks(s):
    return TILE_CHUNKS + (SAMPLE_CHUNKS if s % 2 else 0)


def first_chunk(s):
    return sum(stage_chunks(i) for i in range(s))


def front_steps(f):
    steps = [("norm_in", 0)] + [("in", i) for i in range(W_STEPS["in"])]
    steps += [("conv", 0)] + [("out", i) for i in range(W_STEPS["out"])]
    steps += [("norm_mid", 0)] + [("q", i) for i in range(W_STEPS["q"])]
    steps += [("pick", i) for i in range(HEADS // PG)]
    if f % 2:
        steps += [("sample_pick", 0)]
    return [(name, f, i) for name, i in steps]


def prologue():
    ada = [("ada", 0, i) for i in range(ADA_BLOCKS)]
    rest = ada[ADA_FIRST:]
    steps = ada[:ADA_FIRST] + [("bias", 0, 0)]
    per = len(rest) // W_STEPS["in"]
    for step in front_steps(0):
        steps.append(step)
        if step[0] == "in":
            steps += rest[step[2] * per:(step[2] + 1) * per]
        if step == ("in", 0, W_STEPS["in"] - 1):
            steps.append(("bias", 0, 1))
    return steps


def steps_within(s):
    steps = front_steps(s + 1) if s + 1 < FRONTS else []
    if s == 0:
        steps += [("ada", 1, i) for i in range(ADA_BLOCKS)] + [("bias", 1, 0), ("bias", 1, 1)]
    return steps


def plan(s):
    steps = steps_within(s)
    weight = {"ada": 0.4, "bias": 0.1}
    total = sum(weight.get(name, 1.0) for name, _, _ in steps)
    out, done = [], 0.0
    for step in steps:
        out.append((int(1 + done / total * (TILE_CHUNKS - 4)), step))
        done += weight.get(step[0], 1.0)
    return out


def blocks_of(steps):
    out = []
    for name, f, i in steps:
        if name in W_STEPS or name == "ada":
            out.append((name, f, i))
        elif name == "conv":
            out.append(("pool", f, 0))
        elif name == "norm_mid":
            out.append(("ln1", f, 0))
        elif name == "pick" and i == 0:
            out.append(("keys", f, 0))
    return out


def weight_blocks():
    order = blocks_of(prologue())
    for s in range(FRONTS):
        order += blocks_of(steps_within(s)) + [("ln2", s, 0)]
    return order


def build_trunk(nc, x, xs, small, w_ada, w_in, w_out, w_q, keys, pool_w, ln1, ln2, conv_st, pool_st, uv,
                y, ys, st_new, bounce):
    BLOCKS = weight_blocks()
    AT = {b: n for n, b in enumerate(BLOCKS)}

    ctx = ExitStack()
    with ctx:
        def sb(name, shape, dt=F32):
            return ctx.enter_context(nc.sbuf_tensor(name, shape, dt))

        def sem(name):
            return ctx.enter_context(nc.semaphore(name))

        ring = sb("ring", [P, RC * KPC, SLOT])
        wring = sb("wring", [P, WSLOTS, BK])
        X = [sb(f"X{g}", [P, D]) for g in range(2)]
        Xs = sb("Xs", [NS, D])
        h2 = [sb(f"h2_{g}", [P, D]) for g in range(2)]
        h2rep = sb("h2rep", [P, D])
        hT = sb("hT", [P, DC, NMAX])
        zT = sb("zT", [P, ZB, NMAX])
        catT = sb("catT", [P, DC, NMAX])
        big0 = sb("big0", [P, CB * (2 * P + HIST)])
        big1 = sb("big1", [P, D])
        uext = sb("uext", [P, CB, 2 + P])
        pext = sb("pext", [P, CB, HIST + P])
        cs = sb("cs", [P, CB, NS, CONV_W])
        ps = sb("ps", [P, CB, NS, HIST + 1])
        sts = sb("sts", [P, ST_OUT])
        mod = [sb(f"mod{l}", [P, 6 * DC, NC9]) for l in range(DEPTH)]
        sm = sb("sm", [P, SMALL])
        csil = sb("csil", [P, DC, 32])
        rows = sb("rows", [P, 2, BW])
        diag = sb("diag", [P, RC, KPC, P])
        act_in = sb("act_in", [P, RC, KPC])
        act_out = sb("act_out", [P, RC, KPC])
        ixs = sb("ixs", [P, RC, KPC], U32)
        idx = [sb(f"idx{g}", [P, HEADS * TOPK], U32) for g in range(2)]
        gates = [sb(f"gates{g}", [P, HEADS * TOPK]) for g in range(2)]
        s_pack = sb("s_pack", [P, 2, TOPK, 2], U32)
        s_ig = sb("s_ig", [P, 4, 2, 2], U32)
        kv = sb("kv", [P, 2 * PG, TOPK])
        ki = sb("ki", [P, 2 * PG, TOPK], U32)
        kf = sb("kf", [P, 2 * PG, TOPK])
        ev = sb("ev", [P, PG, TOPK])
        ei = sb("ei", [P, PG, TOPK], U32)
        ea = sb("ea", [P, PG, TOPK], U32)
        fa = sb("fa", [P, PG, TOPK])
        fb = sb("fb", [P, PG, TOPK])
        e1 = sb("e1", [P, PG * TOPK])
        e2 = sb("e2", [P, PG * TOPK])
        rs = sb("rs", [P, PG])
        hs = sb("hs", [P, DC, NS])
        bn = sb("bn", [P, 2, 6])
        mv = sb("mv", [P, 2])
        ve = sb("ve", [P, 1])
        sd = sb("sd", [P, 1])
        rstd = sb("rstd", [P, 1])
        ident = sb("ident", [P, P])
        iota = sb("iota", [P, TOPK])
        mask = sb("mask", [P, NS])
        pick9 = sb("pick9", [P, NC9])
        inv = sb("inv", [P, CB, TOPK])

        tok = catT[:, :, :].rearrange("p a b -> p (a b)")[:, 0:D]
        toks = h2rep[0:NS, :]
        xns = big1[0:NS, 0:D]
        hsrep = big0[:, 0:D].rearrange("p (c t) -> p c t", c=DC)

        acc = ctx.enter_context(nc.psum_tensor("acc", [P, D], F32))
        scores = [ctx.enter_context(nc.psum_tensor(f"scores{i}", [P, 2 * PG, N_KEYS], F32)) for i in range(2)]
        work = [ctx.enter_context(nc.psum_tensor(f"work{i}", [P, 512], F32)) for i in range(2)]

        consts_in = sem("consts_in")
        state_in = sem("state_in")
        w_landed = [sem(f"w_landed{i}") for i in range(WSLOTS)]
        w_used = [sem(f"w_used{i}") for i in range(WSLOTS)]
        made = sem("made")
        work_full = sem("work_full")
        work_free = sem("work_free")
        dve_done = sem("dve_done")
        silu_done = sem("silu_done")
        mod_raw = sem("mod_raw")
        mod_ready = sem("mod_ready")
        var_ready = sem("var_ready")
        std_ready = sem("std_ready")
        xn_ready = sem("xn_ready")
        hT_ready = sem("hT_ready")
        hs_raw = sem("hs_raw")
        hs_ready = sem("hs_ready")
        z_ready = sem("z_ready")
        pooled_ready = sem("pooled_ready")
        cat_ready = sem("cat_ready")
        mT_ready = sem("mT_ready")
        ms_ready = sem("ms_ready")
        tok_ready = sem("tok_ready")
        h2_ready = sem("h2_ready")
        rep_ready = sem("rep_ready")
        q_ready = sem("q_ready")
        scores_ready = sem("scores_ready")
        scores_free = sem("scores_free")
        exp_in = sem("exp_in")
        exp_done = sem("exp_done")
        picks_ready = sem("picks_ready")
        pack_ready = sem("pack_ready")
        pack_out = sem("pack_out")
        spread = sem("spread")
        states_made = sem("states_made")
        ix_staged = sem("ix_staged")
        gathers_go = sem("gathers_go")
        uv_landed = [sem(f"uv_landed{i}") for i in range(RC)]
        acts_ready = sem("acts_ready")
        gelu_ready = sem("gelu_ready")
        diag_ready = sem("diag_ready")
        chunk_used = sem("chunk_used")
        acc_free = sem("acc_free")
        g2_ready = sem("g2_ready")
        x_ready = sem("x_ready")
        stored = sem("stored")

        def wslot(n):
            return wring[:, n % WSLOTS, :]

        def arrived(eng, n):
            eng.wait_ge(w_landed[n % WSLOTS], 16 * (n // WSLOTS + 1))
            return wslot(n)

        def over_chunks(eng, s, lo, hi, body):
            def place(c):
                return (first_chunk(s) + c) % RC, (first_chunk(s) + c) // RC + 1

            g = lo
            while g < hi and place(g)[0]:
                body(g, *place(g))
                g += 1
            turns = (hi - g) // RC
            if turns > 1:
                with eng.Fori(0, turns) as t:
                    for r in range(RC):
                        body(t * RC + (g + r), r, t + place(g)[1])
                g += turns * RC
            while g < hi:
                body(g, *place(g))
                g += 1

        def run_stage(eng, s, first, body, last, steps):
            over_chunks(eng, s, 0, 1, first)
            at = 1
            for after, (name, f, i) in plan(s):
                over_chunks(eng, s, at, max(at, after), body)
                at = max(at, after)
                steps[name](f, i)
            over_chunks(eng, s, at, TILE_CHUNKS - 1, body)
            over_chunks(eng, s, TILE_CHUNKS - 1, TILE_CHUNKS, last)

        block = ctx.enter_context(nc.Block())

        @block.sync
        def _(sp):
            sp.dma_start(sm[:, :], small).then_inc(consts_in, 16)
            sp.dma_start(X[0][:, :], x[0:P, :]).then_inc(consts_in, 16)
            sp.dma_start(X[1][:, :], x[P:2 * P, :]).then_inc(consts_in, 16)
            sp.dma_start(Xs[:, :], xs).then_inc(consts_in, 16)
            stores = 0

            def load(n):
                kind, f, i = BLOCKS[n]
                layer = f if kind == "ada" else f // 2
                src = {"ada": w_ada, "in": w_in, "out": w_out, "q": w_q}.get(kind)
                if n >= WSLOTS:
                    sp.wait_ge(w_used[n % WSLOTS], n // WSLOTS)
                dst = wslot(n)
                if src is not None:
                    src = src[layer, i]
                elif kind == "keys":
                    src = keys[layer]
                elif kind == "pool":
                    dst, src = dst[:, 0:CB * P], pool_w[layer]
                else:
                    src = (ln1 if kind == "ln1" else ln2)[layer:layer + 1, :].broadcast_to([P, 2 * D])
                sp.dma_start(dst, src).then_inc(w_landed[n % WSLOTS], 16)

            n = 0
            for f in range(FRONTS):
                layer = f // 2
                if f % 2 == 1:
                    if layer:
                        sp.wait_ge(states_made, layer)
                    sp.dma_start(cs[:, :, :, :], conv_st[layer]).then_inc(state_in, 16)
                    sp.dma_start(ps[:, :, :, :], pool_st[layer]).then_inc(state_in, 16)
                while BLOCKS[n] != ("q", f, 2):
                    load(n)
                    n += 1
                if f % 2 == 1:
                    sp.wait_ge(states_made, layer + 1)
                    sp.dma_start(st_new[layer], sts[:, :]).then_inc(stored, 16)
                    stores += 1
            while n < len(BLOCKS):
                load(n)
                n += 1
            sp.wait_ge(x_ready, 1)
            sp.dma_start(y[0:P, :], X[0][:, :]).then_inc(stored, 16)
            sp.wait_ge(x_ready, 2)
            sp.dma_start(y[P:2 * P, :], X[1][:, :]).then_inc(stored, 16)
            sp.wait_ge(x_ready, 3)
            sp.dma_start(ys, Xs[:, :]).then_inc(stored, 16)
            sp.wait_ge(stored, 16 * (stores + 3))

        @block.gpsimd
        def _(pool):
            n_made = 0

            def make(ins):
                nonlocal n_made
                n_made += 1
                ins.then_inc(made, 1)
                pool.wait_ge(made, n_made)

            make(nc.gpsimd.memset(ident[:, :], 0.0))
            make(nc.gpsimd.affine_select(out=ident[:, :], in_=ident[:, :], compare_op=ALU.not_equal, fill=1.0,
                                         base=0, pattern=[[-1, P]], channel_multiplier=1))
            make(nc.gpsimd.iota(iota[:, :], [[1, TOPK]], base=0, channel_multiplier=0,
                                allow_small_or_imprecise_dtypes=True))
            make(nc.gpsimd.memset(mask[:, :], 1.0))
            make(nc.gpsimd.affine_select(out=mask[:, :], in_=mask[:, :], compare_op=ALU.is_ge, fill=0.0,
                                         base=0, pattern=[[-TOPK, NS]], channel_multiplier=1))
            make(nc.gpsimd.affine_select(out=mask[:, :], in_=mask[:, :], compare_op=ALU.is_ge, fill=0.0,
                                         base=TOPK - 1, pattern=[[TOPK, NS]], channel_multiplier=-1))
            make(nc.gpsimd.memset(csil[:, :, :], 0.0))
            make(nc.gpsimd.memset(pick9[:, :], 0.0))
            for q in range(4):
                make(nc.gpsimd.affine_select(out=pick9[:, :], in_=pick9[:, :], compare_op=ALU.not_equal, fill=1.0,
                                             base=-32 * q, pattern=[[-1, NC9]], channel_multiplier=1))
            for b, w in enumerate(WINDOWS):
                make(nc.gpsimd.memset(inv[:, b, :], 1.0 / w))
            for t in range(HIST):
                b = min(b for b, w in enumerate(WINDOWS) if w > t + 1)
                make(nc.gpsimd.memset(inv[:, b:CB, t:t + 1], 1.0 / (t + 1)))

            def gather(s, rows):
                G0 = first_chunk(s)

                def body(c, r, n):
                    if not isinstance(c, int) or G0 + c >= RC:
                        pool.wait_ge(chunk_used, c + (G0 - RC + 1))
                    out, src = rows(c, ixs[:, r, :])
                    nc.gpsimd.tensor_copy(out, src).then_inc(ix_staged, 1)
                    pool.wait_ge(ix_staged, c + (G0 + 1))
                    pool.sem_inc(gathers_go, 1)
                    for j in range(KPC):
                        nc.gpsimd.indirect_dma_start(ring[:, r * KPC + j, :], None, uv,
                                                     bass.IndirectOffsetOnAxis(ixs[:, r, j:j + 1], 0))\
                            .then_inc(uv_landed[r], 16)
                return body

            for s in range(FRONTS):
                body = gather(s, lambda c, to, g=s % 2: (to, idx[g][:, bass.ds(c * KPC, KPC)]))
                per = TILE_CHUNKS // (HEADS // PG)
                for i in range(HEADS // PG):
                    pool.wait_ge(picks_ready, s * (HEADS // PG) + i + 1)
                    lo = i * per
                    if s == 0 and i == 0:
                        over_chunks(pool, s, 0, RC, body)
                        lo = RC
                    over_chunks(pool, s, lo, (i + 1) * per, body)
                if s % 2:
                    pool.wait_ge(spread, 16 * (s // 2 + 1))
                    for c in range(TILE_CHUNKS, TILE_CHUNKS + SAMPLE_CHUNKS):
                        q = (c - TILE_CHUNKS) * KPC // 2
                        body = gather(s, lambda c, to, q=q: (to.rearrange("p (q g) -> p q g", g=2),
                                                             s_ig[:, q:q + KPC // 2, 0, :]))
                        over_chunks(pool, s, c, c + 1, body)

        @block.scalar
        def _(act):
            item = [0]

            def drain(*copies):
                act.wait_ge(work_full, item[0] + 1)
                bank = work[item[0] % 2]
                for out, pick, scale, bias in copies[:-1]:
                    nc.scalar.activation(out, pick(bank), ACT.Identity, bias=bias, scale=scale)
                out, pick, scale, bias = copies[-1]
                last = nc.scalar.activation(out, pick(bank), ACT.Identity, bias=bias, scale=scale)
                last.then_inc(work_free, 1)
                item[0] += 1
                return item[0]

            def after_drain(sig):
                act.wait_ge(work_free, item[0])
                act.sem_inc(sig, 1)

            def cols(lo, hi, parts=P):
                return lambda bank: bank[0:parts, lo:hi]

            def root(parts=P, n=[0]):
                n[0] += 1
                act.wait_ge(var_ready, n[0])
                nc.scalar.activation(sd[0:parts, :], ve[0:parts, :], ACT.Sqrt).then_inc(std_ready, 1)

            def transposed(m, shift, scale, with_samples):
                for half in range(2):
                    drain(*[(hT[:, half * 4 + c, 0:P], cols(c * P, (c + 1) * P),
                             m[:, scale + half * 4 + c, 0:1], m[:, shift + half * 4 + c, 0:1])
                            for c in range(4)])
                after_drain(hT_ready)
                if with_samples:
                    drain((hs[:, :, :].rearrange("p a b -> p (a b)"), cols(0, DC * NS), 1.0, 0.0))
                    after_drain(hs_raw)

            def norm_in(f, _):
                smp = f % 2
                root()
                if smp:
                    root(NS)
                act.wait_ge(mod_ready, 2 * (f // 2) + 1)
                transposed(mod[f // 2], SH1, SC1, smp)

            def channel_blocks(f, i, out, scales=None, sig=None):
                n = P + NS * (f % 2)
                for c in (2 * i, 2 * i + 1):
                    drain((out[:, c, 0:n], cols(0, n), 1.0, 0.0))
                if sig is not None:
                    after_drain(sig)

            def dense_in(f, i):
                channel_blocks(f, i, zT, sig=z_ready if i == W_STEPS["in"] - 1 else None)

            def dense_q(f, i):
                channel_blocks(f, i, zT, sig=q_ready)

            def conv(f, _):
                l = f // 2
                n = P + NS * (f % 2)
                for g in range(CB):
                    drain((catT[:, CB + g, 0:n], cols(0, n), sm[:, PSC + l * CB + g:PSC + l * CB + g + 1], 0.0))
                after_drain(cat_ready)

            def dense_out(f, i):
                m = mod[f // 2]
                act.wait_ge(mod_ready, 2 * (f // 2) + 2)
                for c in (2 * i, 2 * i + 1):
                    copies = [(hT[:, c, 0:P], cols(0, P), m[:, G1 + c, 0:1], 0.0)]
                    if f % 2:
                        copies.append((hT[:, c, P:NMAX], cols(P, NMAX), 1.0, 0.0))
                    drain(*copies)
                if i == W_STEPS["out"] - 1:
                    after_drain(mT_ready)

            def norm_mid(f, _):
                m, smp = mod[f // 2], f % 2
                for half in range(2):
                    drain((tok[:, half * 512:(half + 1) * 512], cols(0, 512), 1.0, 0.0))
                if smp:
                    for half in range(2):
                        drain((toks[:, half * 512:(half + 1) * 512], cols(0, 512, NS), 1.0, 0.0))
                after_drain(tok_ready)
                root()
                root()
                if smp:
                    root(NS)
                    root(NS)
                transposed(m, SH2, SC2, smp)
                for half in range(2):
                    drain((h2[f % 2][:, half * 512:(half + 1) * 512], cols(0, 512), 1.0, 0.0))
                if smp:
                    for half in range(2):
                        drain((h2rep[:, half * 512:(half + 1) * 512], cols(0, 512), 1.0, 0.0))
                after_drain(h2_ready)

            n_exp = [0]

            def pick(f, i):
                n_exp[0] += 1
                act.wait_ge(exp_in, n_exp[0])
                nc.scalar.activation(kv[:, 0:PG, :], kv[:, 0:PG, :], ACT.Exp).then_inc(exp_done, 1)

            def sample_pick(f, i):
                pick(f, i)
                act.wait_ge(pack_ready, f // 2 + 1)
                for q in range(4):
                    act.dma_start(bounce[q].rearrange("a t x -> t a x"),
                                  s_pack[32 * q:32 * q + NS, :, :, :].rearrange("p a k g -> p a (k g)"))\
                        .then_inc(pack_out, 16)
                act.wait_ge(pack_out, 64 * (f // 2 + 1))
                act.dma_start(s_ig[:, :, :, :].rearrange("p q a g -> p (q a) g"),
                              bounce.rearrange("q a t (k g) -> (t k) (q a) g", g=2)).then_inc(spread, 16)

            def ada(layer, i):
                drain((rows[:, i % 2, :], cols(0, BW), 1.0, 0.0))
                drain((mod[layer][:, 2 * i:2 * i + 2, :].rearrange("p a b -> p (a b)"), cols(0, 2 * NC9), 1.0, 0.0))
                if i in (ADA_FIRST - 1, ADA_BLOCKS - 1):
                    after_drain(mod_raw)

            steps = {"norm_in": norm_in, "in": dense_in, "conv": conv, "out": dense_out, "norm_mid": norm_mid,
                     "q": dense_q, "pick": pick, "sample_pick": sample_pick, "ada": ada, "bias": lambda l, i: None}

            def gelu(s):
                G0 = first_chunk(s)

                def body(c, r, n):
                    act.wait_ge(acts_ready, c + (G0 + 1))
                    nc.scalar.activation(act_out[:, r, :], act_in[:, r, :], ACT.Gelu).then_inc(gelu_ready, 1)
                return body

            def gate2(f, parts):
                out = tok if parts == P else toks
                for half in range(2):
                    drain((out[:, half * 512:(half + 1) * 512], cols(0, 512, parts), 1.0, 0.0))
                after_drain(g2_ready)
                root(parts)

            act.wait_ge(consts_in, 16 * 4)
            act.wait_ge(made, 7)
            nc.scalar.activation(csil[:, :, 0:NC9], sm[:, COND:SMALL].rearrange("p (k r) -> p k r", k=DC),
                                 ACT.Silu).then_inc(silu_done, 1)
            for name, f, i in prologue():
                steps[name](f, i)
            for s in range(FRONTS):
                body = gelu(s)
                run_stage(act, s, body, body, body, steps)
                if s % 2:
                    gate2(s, P)
                    for c in range(TILE_CHUNKS, TILE_CHUNKS + SAMPLE_CHUNKS):
                        over_chunks(act, s, c, c + 1, body)
                    gate2(s, NS)
                else:
                    gate2(s, P)

        @block.vector
        def _(dve):
            counts = {}

            def link(ins, sig=dve_done):
                counts[id(sig)] = counts.get(id(sig), 0) + 1
                ins.then_inc(sig, 1)
                dve.wait_ge(sig, counts[id(sig)])

            roots = [0]

            def normalise(src, out, parts=P, sig=dve_done):
                for i in range(2):
                    last = nc.vector.bn_stats(bn[0:parts, i, :], src[:, i * 512:(i + 1) * 512])
                link(last)
                link(nc.vector.bn_aggr(mv[0:parts, :], bn[0:parts, :, :].rearrange("p a b -> p (a b)")))
                nc.vector.tensor_scalar(ve[0:parts, :], mv[0:parts, 1:2], EPS, None, ALU.add).then_inc(var_ready, 1)
                roots[0] += 1
                dve.wait_ge(std_ready, roots[0])
                link(nc.vector.reciprocal(rstd[0:parts, :], sd[0:parts, :]))
                link(nc.vector.tensor_scalar(out, src, mv[0:parts, 0:1], rstd[0:parts, 0:1], ALU.subtract, ALU.mult),
                     sig)

            def gain(t, n, parts=P, sig=dve_done, inc=1):
                gb = arrived(dve, n)
                link(nc.vector.tensor_tensor(t, t, gb[0:parts, 0:D], ALU.mult))
                return nc.vector.tensor_tensor(t, t, gb[0:parts, D:2 * D], ALU.add)

            def modulate_samples(f, shift, scale):
                m = mod[f // 2]
                link(nc.vector.tensor_tensor(hs[:, :, :], hs[:, :, :], m[:, scale:scale + DC, 1:NC9], ALU.mult))
                link(nc.vector.tensor_tensor(hT[:, :, P:NMAX], hs[:, :, :], m[:, shift:shift + DC, 1:NC9], ALU.add),
                     hs_ready)

            def norm_in(f, _):
                smp = f % 2
                normalise(X[f % 2][:, :], h2[f % 2][:, :], P, xn_ready)
                if smp:
                    normalise(Xs[:, :], xns, NS, xn_ready)
                    dve.wait_ge(hs_raw, f // 2 * 2 + 1)
                    modulate_samples(f, SH1, SC1)

            def conv_weight(l, b, k):
                at = CONV + (l * CB + b) * CONV_W + k
                return sm[:, at:at + 1]

            def conv(f, _):
                l, smp = f // 2, f % 2
                if f % 2 == 0:
                    nc.vector.memset(uext[:, :, 0:2], 0.0)
                    link(nc.vector.memset(pext[:, :, 0:HIST], 0.0))
                else:
                    nc.vector.tensor_copy(uext[:, :, 0:2], uext[:, :, P:P + 2])
                    link(nc.vector.tensor_copy(pext[:, :, 0:HIST], pext[:, :, P:P + HIST]))
                dve.wait_ge(z_ready, f + 1)
                nc.vector.tensor_tensor(uext[:, :, 2:2 + P], zT[:, CB:2 * CB, 0:P], zT[:, 2 * CB:3 * CB, 0:P], ALU.mult)
                link(nc.vector.tensor_copy(pext[:, :, HIST:HIST + P], zT[:, 3 * CB:ZB, 0:P]))
                yT = big0[:, 0:CB * P].rearrange("p (b t) -> p b t", b=CB)
                s0 = big1[:, 0:CB * (HIST + P)].rearrange("p (b t) -> p b t", b=CB)
                s1 = big0[:, CB * P:CB * P + CB * (HIST + P)].rearrange("p (b t) -> p b t", b=CB)
                E = HIST + P
                for b in range(CB):
                    nc.vector.tensor_scalar(yT[:, b, :], uext[:, b, 0:P], conv_weight(l, b, 0), None, ALU.mult)
                link(nc.vector.tensor_tensor(s0[:, :, 1:E], pext[:, :, 1:E], pext[:, :, 0:E - 1], ALU.add))
                for b in range(CB):
                    nc.vector.scalar_tensor_tensor(yT[:, b, :], uext[:, b, 1:1 + P], conv_weight(l, b, 1),
                                                   yT[:, b, :], ALU.mult, ALU.add)
                link(nc.vector.tensor_tensor(s1[:, 1:CB, 3:E], s0[:, 1:CB, 3:E], s0[:, 1:CB, 1:E - 2], ALU.add))
                for b in range(CB):
                    nc.vector.scalar_tensor_tensor(yT[:, b, :], uext[:, b, 2:2 + P], conv_weight(l, b, 2),
                                                   yT[:, b, :], ALU.mult, ALU.add)
                link(nc.vector.tensor_tensor(s0[:, 2:CB, 7:E], s1[:, 2:CB, 7:E], s1[:, 2:CB, 3:E - 4], ALU.add))
                nc.vector.tensor_tensor(catT[:, 0:CB, 0:P], zT[:, 0:CB, 0:P], yT, ALU.mult)
                link(nc.vector.tensor_tensor(s1[:, 3:CB, HIST:E], s0[:, 3:CB, HIST:E], s0[:, 3:CB, 7:E - 8], ALU.add))
                for b, w in enumerate(WINDOWS):
                    last = nc.vector.scalar_tensor_tensor(zT[:, 3 * CB + b, 0:P], (s0, s1)[b % 2][:, b, HIST:E], 1.0 / w,
                                                          pext[:, b, HIST:E], ALU.mult, ALU.subtract)
                if f % 2 == 0:
                    link(last)
                    for b in range(CB):
                        last = nc.vector.tensor_tensor(zT[:, 3 * CB + b, 0:TOPK], (s0, s1)[b % 2][:, b, HIST:HIST + TOPK],
                                                       inv[:, b, :], ALU.mult)
                    link(last)
                    last = nc.vector.tensor_tensor(zT[:, 3 * CB:ZB, 0:TOPK], zT[:, 3 * CB:ZB, 0:TOPK],
                                                   pext[:, :, HIST:HIST + TOPK], ALU.subtract)
                if smp:
                    link(last)
                    dve.wait_ge(state_in, 32 * (l + 1))
                    nc.vector.tensor_tensor(cs[:, :, :, 2:3].rearrange("p b t o -> p b (t o)"),
                                            zT[:, CB:2 * CB, P:NMAX], zT[:, 2 * CB:3 * CB, P:NMAX], ALU.mult)
                    link(nc.vector.tensor_copy(ps[:, :, :, HIST:HIST + 1].rearrange("p b t o -> p b (t o)"),
                                               zT[:, 3 * CB:ZB, P:NMAX]))
                    ysT = big0[:, 0:CB * NS].rearrange("p (b t) -> p b t", b=CB)
                    sw = big0[:, CB * NS:2 * CB * NS].rearrange("p (b t) -> p b t", b=CB)
                    for b, w in enumerate(WINDOWS):
                        nc.vector.tensor_scalar(ysT[:, b, :], cs[:, b, :, 0], conv_weight(l, b, 0), None, ALU.mult)
                        last = nc.vector.tensor_reduce(sw[:, b, :], ps[:, b, :, HIST + 1 - w:HIST + 1], AX.X, ALU.add)
                    link(last)
                    for k in (1, 2):
                        for b in range(CB):
                            last = nc.vector.scalar_tensor_tensor(ysT[:, b, :], cs[:, b, :, k], conv_weight(l, b, k),
                                                                  ysT[:, b, :], ALU.mult, ALU.add)
                        link(last)
                    for b, w in enumerate(WINDOWS):
                        nc.vector.scalar_tensor_tensor(zT[:, 3 * CB + b, P:NMAX], sw[:, b, :], 1.0 / w, ps[:, b, :, HIST],
                                                       ALU.mult, ALU.subtract)
                    last = nc.vector.tensor_tensor(catT[:, 0:CB, P:NMAX], zT[:, 0:CB, P:NMAX], ysT, ALU.mult)
                link(last, pooled_ready)
                if smp:
                    if l:
                        dve.wait_ge(stored, 16 * l)
                    nc.vector.tensor_copy(sts[:, O_CP:O_PP].rearrange("p (b k) -> p b k", b=CB), uext[:, :, P:P + 2])
                    nc.vector.tensor_copy(sts[:, O_PP:O_CS].rearrange("p (b k) -> p b k", b=CB), pext[:, :, P:P + HIST])
                    nc.vector.tensor_copy(sts[:, O_CS:O_PS].rearrange("p (b t k) -> p (b t) k", b=CB, t=NS),
                                          cs[:, :, :, 1:3].rearrange("p b t k -> p (b t) k"))
                    nc.vector.tensor_copy(sts[:, O_PS:ST_OUT].rearrange("p (b t k) -> p (b t) k", b=CB, t=NS),
                                          ps[:, :, :, 1:HIST + 1].rearrange("p b t k -> p (b t) k"))\
                        .then_inc(states_made, 1)

            def norm_mid(f, _):
                l, smp = f // 2, f % 2
                if smp:
                    dve.wait_ge(mT_ready, f + 1)
                    link(nc.vector.tensor_tensor(hT[:, :, P:NMAX], hT[:, :, P:NMAX], mod[l][:, G1:G1 + DC, 1:NC9],
                                                 ALU.mult), ms_ready)
                xt = X[f % 2][:, :]
                dve.wait_ge(tok_ready, f + 1)
                link(nc.vector.scalar_tensor_tensor(xt, xt, ALPHA, tok, ALU.mult, ALU.add))
                normalise(xt, xt)
                n = AT["ln1", f, 0]
                last = gain(xt, n)
                if not smp:
                    last.then_inc(w_used[n % WSLOTS], 1)
                    dve.wait_ge(w_used[n % WSLOTS], n // WSLOTS + 1)
                else:
                    link(last)
                normalise(xt, h2[f % 2][:, :], P, xn_ready)
                if smp:
                    xt = Xs[:, :]
                    link(nc.vector.scalar_tensor_tensor(xt, xt, ALPHA, toks, ALU.mult, ALU.add))
                    normalise(xt, xt, NS)
                    last = gain(xt, n, NS)
                    last.then_inc(w_used[n % WSLOTS], 1)
                    dve.wait_ge(w_used[n % WSLOTS], n // WSLOTS + 1)
                    normalise(xt, xns, NS, xn_ready)
                    dve.wait_ge(hs_raw, f // 2 * 2 + 2)
                    modulate_samples(f, SH2, SC2)
                    for c in range(DC):
                        last = nc.vector.tensor_copy(hsrep[:, c, :].rearrange("p (t k) -> p t k", k=TOPK),
                                                     hT[:, c, P:NMAX].unsqueeze(2).broadcast_to([P, NS, TOPK]))
                    link(last, rep_ready)

            def search(src, tmp, values, places, free=None):
                n = src.shape[1]
                for i in range(n):
                    last = nc.vector.max(values[:, i, 0:8], src[:, i, :])
                link(last)
                for i in range(n):
                    nc.vector.max_index(places[:, i, 0:8], values[:, i, 0:8], src[:, i, :])
                    last = nc.vector.match_replace(tmp[:, i, :], values[:, i, 0:8], src[:, i, :], MINUS)
                link(last, free or dve_done)
                for i in range(n):
                    last = nc.vector.max(values[:, i, 8:16], tmp[:, i, :])
                link(last)
                for i in range(n):
                    last = nc.vector.max_index(places[:, i, 8:16], values[:, i, 8:16], tmp[:, i, :])
                link(last)

            n_scores = [0]

            def search_pairs():
                nh = PG
                now = scores[n_scores[0] % 2]
                n_scores[0] += 1
                dve.wait_ge(scores_ready, n_scores[0])
                search(now, big0[:, 0:2 * nh * N_KEYS].rearrange("p (i k) -> p i k", k=N_KEYS), kv, ki, scores_free)
                nc.vector.tensor_copy(kf[:, :, :], ki[:, :, :])
                pairs = big1[:, 0:nh * 256].rearrange("p (h i j) -> p h i j", h=nh, i=TOPK)
                v4 = kv[:, :, :].rearrange("p (h s) k -> p h s k", s=2)
                one = v4[:, :, 0, :].unsqueeze(3).broadcast_to([P, nh, TOPK, TOPK])
                two = v4[:, :, 1, :].unsqueeze(2).broadcast_to([P, nh, TOPK, TOPK])
                link(nc.vector.tensor_tensor(pairs, one, two, ALU.add))
                tmp = big0[:, 0:nh * 256].rearrange("p (i k) -> p i k", k=256)
                search(big1[:, 0:nh * 256].rearrange("p (i k) -> p i k", k=256), tmp, ev, ei)

            n_exp = [0]

            def decode(f, number, gate, sig):
                l, nh = f // 2, PG
                n = nh * TOPK
                ex = kv[:, 0:nh, :]
                link(nc.vector.tensor_tensor(ex, ev[:, 0:nh, :],
                                             ev[:, 0:nh, 0:1].broadcast_to([P, nh, TOPK]), ALU.subtract), exp_in)
                link(nc.vector.tensor_scalar(ea[:, 0:nh, :], ei[:, 0:nh, :], 4, None, ALU.logical_shift_right))
                link(nc.vector.tensor_copy(fa[:, 0:nh, :], ea[:, 0:nh, :]))
                link(nc.vector.tensor_scalar(ea[:, 0:nh, :], ei[:, 0:nh, :], TOPK - 1, None, ALU.bitwise_and))
                link(nc.vector.tensor_copy(fb[:, 0:nh, :], ea[:, 0:nh, :]))
                k4 = kf[:, 0:2 * nh, :].rearrange("p (h s) k -> p h s k", s=2)
                for place, half, hit, out in ((fa, 0, big0, e1), (fb, 1, big1, e2)):
                    h3 = hit[:, 0:n * TOPK].rearrange("p (a j) -> p a j", j=TOPK)
                    h4 = hit[:, 0:n * TOPK].rearrange("p (h a j) -> p h a j", h=nh, j=TOPK)
                    flat = place[:, 0:nh, :].rearrange("p h k -> p (h k)").unsqueeze(2).broadcast_to([P, n, TOPK])
                    link(nc.vector.tensor_tensor(h3, flat, iota[:, :].unsqueeze(1).broadcast_to([P, n, TOPK]), ALU.is_equal))
                    link(nc.vector.tensor_tensor(h4, h4, k4[:, :, half, :].unsqueeze(2).broadcast_to([P, nh, TOPK, TOPK]),
                                                 ALU.mult))
                    link(nc.vector.tensor_reduce(out[:, 0:n], h3, AX.X, ALU.add))
                link(nc.vector.scalar_tensor_tensor(e1[:, 0:n], e1[:, 0:n], float(N_KEYS), e2[:, 0:n], ALU.mult, ALU.add))
                nc.vector.tensor_scalar(number, e1[:, :].rearrange("p (h k) -> p h k", k=TOPK), float(l * N_EXPERTS), None, ALU.add)
                n_exp[0] += 1
                dve.wait_ge(exp_done, n_exp[0])
                link(nc.vector.tensor_reduce(rs[:, 0:nh], ex, AX.X, ALU.add))
                link(nc.vector.reciprocal(rs[:, 0:nh], rs[:, 0:nh]))
                link(nc.vector.tensor_tensor(gate, ex, rs[:, 0:nh].unsqueeze(2).broadcast_to([P, nh, TOPK]),
                                             ALU.mult), sig)

            def pick(f, i):
                search_pairs()
                at = slice(i * PG * TOPK, (i + 1) * PG * TOPK)
                decode(f, idx[f % 2][:, at].rearrange("p (h k) -> p h k", k=TOPK),
                       gates[f % 2][:, at].rearrange("p (h k) -> p h k", k=TOPK), picks_ready)

            def sample_pick(f, _):
                search_pairs()
                if f // 2:
                    dve.wait_ge(pack_out, 64 * (f // 2))
                decode(f, s_pack[:, 0, :, :].rearrange("p k h -> p h k"),
                       s_pack[:, 1, :, :].bitcast(F32).rearrange("p k h -> p h k"), pack_ready)

            def bias(layer, part):
                dve.wait_ge(mod_raw, 2 * layer + part + 1)
                m = mod[layer]
                lo, hi = ((SH1, G1), (G1, 6 * DC))[part]
                b = sm[:, B_ADA + layer * 6 * DC + lo:B_ADA + layer * 6 * DC + hi]
                link(nc.vector.tensor_tensor(m[:, lo:hi, :], m[:, lo:hi, :], b.unsqueeze(2).broadcast_to([P, hi - lo, NC9]),
                                             ALU.add))
                sc = (SC1, SC2)[part]
                link(nc.vector.tensor_scalar(m[:, sc:sc + DC, :], m[:, sc:sc + DC, :], 1.0, None, ALU.add), mod_ready)

            def nothing(f, i):
                pass

            steps = {"norm_in": norm_in, "in": nothing, "conv": conv, "out": nothing, "norm_mid": norm_mid,
                     "q": nothing, "pick": pick, "sample_pick": sample_pick, "ada": nothing, "bias": bias}

            def chunk_work(s, gate_of, xt, base, width):
                G0 = first_chunk(s)

                def dots(c, r, n):
                    dve.wait_ge(uv_landed[r], n * (16 * KPC))
                    for j in range(KPC):
                        u = ring[:, r * KPC + j, 0:D]
                        last = nc.vector.scalar_tensor_tensor(u, u, 1.0, xt, ALU.mult, ALU.mult,
                                                              accum_out=act_in[:, r, j:j + 1])
                    last.then_inc(acts_ready, 1)

                def diags(c, r, n=None):
                    dve.wait_ge(gelu_ready, c + (G0 + 1))
                    for j in range(KPC):
                        last = nc.vector.tensor_scalar(diag[:, r, j, 0:width], base[:, 0:width], act_out[:, r, j:j + 1],
                                                       gate_of(c, j), ALU.mult, ALU.mult)
                    last.then_inc(diag_ready, 1)

                def both(c, r, n):
                    dots(c, r, n)
                    diags(c, r, n)

                return dots, diags, both

            gate2s = [0]
            xr = [0]

            def finish(s, parts):
                t = tok if parts == P else toks
                xt = X[s % 2][:, :] if parts == P else Xs[:, :]
                n = AT["ln2", s, 0]
                gate2s[0] += 1
                dve.wait_ge(g2_ready, gate2s[0])
                done = first_chunk(s) + (TILE_CHUNKS if parts == P else stage_chunks(s))
                dve.wait_ge(chunk_used, done)
                link(nc.vector.tensor_tensor(t, t, acc[0:parts, :], ALU.mult), acc_free)
                link(nc.vector.scalar_tensor_tensor(xt, xt, ALPHA, t, ALU.mult, ALU.add))
                normalise(xt, xt, parts)
                last = gain(xt, n, parts)
                if s >= FRONTS - 2:
                    link(last, x_ready)
                    last = None
                if parts == NS or s % 2 == 0:
                    if last is None:
                        last = nc.vector.tensor_copy(ve[0:1, :], mv[0:1, 0:1])
                    last.then_inc(w_used[n % WSLOTS], 1)
                    dve.wait_ge(w_used[n % WSLOTS], n // WSLOTS + 1)
                elif last is not None:
                    link(last)

            dve.wait_ge(made, 12 + len(WINDOWS) + HIST)
            dve.wait_ge(consts_in, 16 * 4)
            for name, f, i in prologue():
                steps[name](f, i)
            for s in range(FRONTS):
                g = s % 2

                def tile_gate(c, j, g=g):
                    return gates[g][:, bass.ds(c * KPC + j, 1)]

                dots, diags, both = chunk_work(s, tile_gate, h2[g][:, :], ident, P)
                run_stage(dve, s, both, both, both, steps)
                if s % 2:
                    def sample_gate(c, j):
                        at = (c - TILE_CHUNKS) * KPC + j
                        return s_ig[:, at // 2, 1, at % 2:at % 2 + 1].bitcast(F32)

                    finish(s, P)
                    dve.wait_ge(spread, 16 * (s // 2 + 1))
                    _, _, both = chunk_work(s, sample_gate, h2rep[:, :], mask, NS)
                    for c in range(TILE_CHUNKS, stage_chunks(s)):
                        over_chunks(dve, s, c, c + 1, both)
                    finish(s, NS)
                else:
                    finish(s, P)

        @block.tensor
        def _(pe):
            item = [0]

            def bank():
                if item[0] >= 2:
                    pe.wait_ge(work_free, item[0] - 1)
                b = work[item[0] % 2]
                item[0] += 1
                return b

            def transposes(src, parts=P):
                for half in range(2):
                    b = bank()
                    for c in range(4):
                        last = nc.tensor.transpose(b[:, c * P:(c + 1) * P], src[:, (half * 4 + c) * P:(half * 4 + c + 1) * P],
                                                   ident[:, :])
                    last.then_inc(work_full, 1)

            def to_channels(f, nth):
                smp = f % 2
                n_xn = [0, 2, 6, 8][f] + (nth * 2 if smp else nth)
                pe.wait_ge(xn_ready, n_xn + 1)
                transposes(h2[f % 2])
                if smp:
                    pe.wait_ge(xn_ready, n_xn + 2)
                    b = bank()
                    for c in range(DC):
                        last = nc.tensor.matmul(b[:, c * NS:(c + 1) * NS], xns[:, c * P:(c + 1) * P], ident[0:NS, 0:NS],
                                                start=True, stop=True)
                    last.then_inc(work_full, 1)
                pe.wait_ge(hT_ready, 2 * f + nth + 1)
                if smp:
                    pe.wait_ge(hs_ready, f // 2 * 2 + nth + 1)

            def to_tokens(f):
                for half in range(2):
                    b = bank()
                    for c in range(4):
                        last = nc.tensor.transpose(b[:, c * P:(c + 1) * P], hT[:, half * 4 + c, 0:P], ident[:, :])
                    last.then_inc(work_full, 1)

            def used(nb):
                pe.wait_ge(work_full, item[0])
                pe.sem_inc(w_used[nb % WSLOTS], 1)

            def dense(kind, f, i, rhs):
                n = P + NS * (f % 2)
                nb = AT[kind, f, i]
                w = arrived(pe, nb).rearrange("p (k c) -> p k c", k=DC)
                for j in range(BW // P):
                    b = bank()
                    for k in range(DC):
                        last = nc.tensor.matmul(b[:, 0:n], w[:, k, j * P:(j + 1) * P], rhs[:, k, 0:n],
                                                start=(k == 0), stop=(k == DC - 1))
                    last.then_inc(work_full, 1)
                used(nb)

            def norm_in(f, _):
                to_channels(f, 0)

            def conv(f, _):
                n = P + NS * (f % 2)
                pe.wait_ge(pooled_ready, f + 1)
                nb = AT["pool", f, 0]
                w = arrived(pe, nb)
                for g in range(CB):
                    b = bank()
                    nc.tensor.matmul(b[:, 0:n], w[:, g * P:(g + 1) * P], zT[:, 3 * CB + g, 0:n], start=True, stop=True)\
                        .then_inc(work_full, 1)
                used(nb)

            def dense_out(f, i):
                pe.wait_ge(cat_ready, f + 1)
                dense("out", f, i, catT)

            def norm_mid(f, _):
                smp = f % 2
                pe.wait_ge(mT_ready, f + 1)
                to_tokens(f)
                if smp:
                    pe.wait_ge(ms_ready, f // 2 + 1)
                    for half in range(2):
                        b = bank()
                        for c in range(4):
                            last = nc.tensor.matmul(b[0:NS, c * P:(c + 1) * P], hT[:, half * 4 + c, P:NMAX], ident[:, :],
                                                    start=True, stop=True)
                        last.then_inc(work_full, 1)
                to_channels(f, 1)
                to_tokens(f)
                if smp:
                    pe.wait_ge(rep_ready, f // 2 + 1)
                    for half in range(2):
                        b = bank()
                        for c in range(4):
                            last = nc.tensor.matmul(b[:, c * P:(c + 1) * P], hsrep[:, half * 4 + c, :], ident[:, :],
                                                    start=True, stop=True)
                        last.then_inc(work_full, 1)

            n_scores = [0]

            def scores_bank():
                if n_scores[0] >= 2:
                    pe.wait_ge(scores_free, n_scores[0] - 1)
                b = scores[n_scores[0] % 2]
                n_scores[0] += 1
                return b

            def pick(f, i):
                pe.wait_ge(q_ready, (f + 1) * W_STEPS["q"])
                nb = AT["keys", f, 0]
                k = (arrived(pe, nb) if i == 0 else wslot(nb)).rearrange("p (i c) -> p i c", c=N_KEYS)
                b = scores_bank()
                for h in range(2 * PG):
                    c = 2 * PG * i + h
                    last = nc.tensor.matmul(b[:, h, :], zT[:, c, 0:P], k[:, c, :], start=True, stop=True)
                last.then_inc(scores_ready, 1)
                if f % 2 == 0 and i == HEADS // PG - 1:
                    pe.wait_ge(scores_ready, n_scores[0])
                    pe.sem_inc(w_used[nb % WSLOTS], 1)

            def sample_pick(f, _):
                nb = AT["keys", f, 0]
                k = wslot(nb).rearrange("p (i c) -> p i c", c=N_KEYS)
                b = scores_bank()
                for g in range(2):
                    for q in range(4):
                        for half in range(2):
                            i = 2 * (4 * g + q) + half
                            last = nc.tensor.matmul(b[32 * q:32 * q + NS, 2 * g + half, :], zT[:, i, P:NMAX],
                                                    k[:, i, :], start=True, stop=True)
                last.then_inc(scores_ready, 1)
                pe.wait_ge(scores_ready, n_scores[0])
                pe.sem_inc(w_used[nb % WSLOTS], 1)

            def ada(layer, i):
                nb = AT["ada", layer, i]
                w = arrived(pe, nb).rearrange("p (k c) -> p k c", k=DC)
                b = bank()
                for k in range(DC):
                    strip = slice(32 * (k % 4), 32 * (k % 4) + 32)
                    last = nc.tensor.matmul(b[strip, 0:BW], csil[:, k, :], w[:, k, :], start=(k < 4), stop=(k >= 4))
                last.then_inc(work_full, 1)
                used(nb)
                pe.wait_ge(work_free, item[0])
                b = bank()
                for j in range(BW // P):
                    last = nc.tensor.matmul(b[:, j * NC9:(j + 1) * NC9], rows[:, i % 2, j * P:(j + 1) * P], pick9[:, :],
                                            start=True, stop=True)
                last.then_inc(work_full, 1)

            steps = {"norm_in": norm_in, "in": lambda f, i: dense("in", f, i, hT), "conv": conv, "out": dense_out,
                     "norm_mid": norm_mid, "q": lambda f, i: dense("q", f, i, hT), "pick": pick,
                     "sample_pick": sample_pick, "ada": ada, "bias": lambda l, i: None}

            def summing(s, width):
                G0 = first_chunk(s)

                def body(c, r, n, first=False, last_one=False):
                    pe.wait_ge(diag_ready, c + (G0 + 1))
                    for j in range(KPC):
                        for half in range(2):
                            last = nc.tensor.matmul(acc[0:width, half * 512:(half + 1) * 512], diag[:, r, j, 0:width],
                                                    ring[:, r * KPC + j, D + half * 512:D + (half + 1) * 512],
                                                    start=(first and j == 0), stop=(last_one and j == KPC - 1))
                    last.then_inc(chunk_used, 1)
                return body

            def gate2(s, parts):
                m = mod[s // 2]
                for half in range(2):
                    b = bank()
                    for c in range(4):
                        col = m[:, G2 + half * 4 + c, 0:1].broadcast_to([P, P]) if parts == P else m[:, G2 + half * 4 + c, 1:NC9]
                        last = nc.tensor.matmul(b[0:parts, c * P:(c + 1) * P], col, ident[:, :], start=True, stop=True)
                    last.then_inc(work_full, 1)

            pe.wait_ge(made, 12)
            pe.wait_ge(consts_in, 16 * 4)
            pe.wait_ge(silu_done, 1)
            for name, f, i in prologue():
                steps[name](f, i)
            accs = [0]
            for s in range(FRONTS):
                body = summing(s, P)
                if accs[0]:
                    pe.wait_ge(acc_free, accs[0])
                run_stage(pe, s, lambda c, r, n: body(c, r, n, first=True), body,
                          lambda c, r, n: body(c, r, n, last_one=True), steps)
                accs[0] += 1
                gate2(s, P)
                if s % 2:
                    body = summing(s, NS)
                    pe.wait_ge(acc_free, accs[0])
                    for c in range(SAMPLE_CHUNKS):
                        g = TILE_CHUNKS + c
                        over_chunks(pe, s, g, g + 1, lambda *at, c=c: body(*at, first=(c == 0),
                                                                           last_one=(c == SAMPLE_CHUNKS - 1)))
                    accs[0] += 1
                    gate2(s, NS)


def kernel(x_prompt, x_sample, state_conv, state_pool, c_prompt, c_sample, w_ada, b_ada, w_in, conv_w, pool_w,
           pool_scale, w_out, ln1_g, ln1_b, w_q, sub_keys, u_experts, v_experts, ln2_g, ln2_b):
    import concourse.bacc as _bacc
    from concourse.bass_utils import run_bass_kernel_spmd as _run

    a = {k: np.asarray(v) for k, v in locals().items() if not k.startswith("_")}

    def blocks(w):
        n = w.shape[2] // BW
        return np.ascontiguousarray(w.reshape(DEPTH, DC, P, n, BW).transpose(0, 3, 2, 1, 4)).reshape(DEPTH, n, P, BK)

    def per_channel(v, lead):
        v = v.reshape(*lead, -1, P)
        return np.moveaxis(v, -1, 0)

    cond = per_channel(np.concatenate([a["c_prompt"], a["c_sample"]]), (NC9,))
    small = np.concatenate([
        per_channel(a["b_ada"], (DEPTH,)).reshape(P, -1),
        per_channel(a["conv_w"], (DEPTH, CONV_W)).transpose(0, 1, 3, 2).reshape(P, -1),
        per_channel(a["pool_scale"], (DEPTH,)).reshape(P, -1),
        cond.transpose(0, 2, 1).reshape(P, -1)], axis=1)

    def states(s, width):
        s = per_channel(s, s.shape[:3]).transpose(1, 0, 4, 2, 3)
        return np.ascontiguousarray(np.concatenate([s, np.zeros(s.shape[:4] + (1,), s.dtype)], axis=4))

    arrays = {
        "x": a["x_prompt"].reshape(SEQ, D), "xs": a["x_sample"].reshape(NS, D), "small": small,
        "w_ada": blocks(a["w_ada"]), "w_in": blocks(a["w_in"]), "w_out": blocks(a["w_out"]), "w_q": blocks(a["w_q"]),
        "keys": a["sub_keys"].transpose(0, 4, 1, 2, 3).reshape(DEPTH, P, HP * N_KEYS),
        "pool_w": a["pool_w"].transpose(0, 2, 1, 3).reshape(DEPTH, P, CB * P),
        "ln1": np.concatenate([a["ln1_g"], a["ln1_b"]], axis=1), "ln2": np.concatenate([a["ln2_g"], a["ln2_b"]], axis=1),
        "conv_st": states(a["state_conv"], 3), "pool_st": states(a["state_pool"], 16),
        "uv": np.concatenate([a["u_experts"].reshape(-1, D), a["v_experts"].reshape(-1, D)], axis=1),
    }
    arrays = {f"in_{k}": np.ascontiguousarray(v) for k, v in arrays.items()}
    outs = {"y": (SEQ, D), "ys": (NS, D), "st_new": (DEPTH, P, ST_OUT)}

    nc = _bacc.Bacc("TRN2", target_bir_lowering=False, num_devices=1)
    ins = [nc.dram_tensor(k, v.shape, F32, kind="ExternalInput").ap() for k, v in arrays.items()]
    out = [nc.dram_tensor(f"out_{k}", v, F32, kind="ExternalOutput").ap() for k, v in outs.items()]
    bounce = nc.dram_tensor("bounce", (4, 2, NS, 2 * TOPK), U32, kind="Internal").ap()
    build_trunk(nc, *ins, *out, bounce)
    r = _run(nc, [arrays], core_ids=[0]).results[0]

    st = r["out_st_new"]

    def rows(part, *dims):
        v = part.reshape(DEPTH, P, CB, *dims)
        return np.moveaxis(v, (2, 1), (-2, -1)).reshape(DEPTH, *dims, CB * P)

    return (r["out_y"].reshape(1, SEQ, D), r["out_ys"].reshape(NS, 1, D),
            rows(st[:, :, O_CP:O_PP], 1, 2), rows(st[:, :, O_PP:O_CS], 1, HIST),
            rows(st[:, :, O_CS:O_PS], NS, 2), rows(st[:, :, O_PS:ST_OUT], NS, HIST))
```

```python
import numpy as np
import concourse.bass as bass
from concourse import mybir
from contextlib import ExitStack

F32 = mybir.dt.float32
U32 = mybir.dt.uint32
ALU = mybir.AluOpType
ACT = mybir.ActivationFunctionType
AX = mybir.AxisListType

D = 1024
DEPTH = 2
SEQ = 256
NS = 8
CONV_W = 3
WINDOWS = (2, 4, 8, 16)
HIST = max(WINDOWS) - 1
HEADS = 8
N_KEYS = 128
N_EXPERTS = N_KEYS * N_KEYS
TOPK = 16
ALPHA = float((2 * DEPTH) ** 0.25)
EPS = 1e-5

P = 128
DC = D // P
CB = D // 2 // P
ZB = 4 * CB
HP = 2 * HEADS
NC9 = 1 + NS
NMAX = P + NS
BW = 256
BK = DC * BW
WSLOTS = 4
WORKS = 3
KPC = 2
RC = 6
SLOT = 2 * D
TILE_CHUNKS = HEADS * TOPK // KPC
SAMPLE_CHUNKS = HEADS * NS * TOPK // P // KPC
PG = 2
SH1, SC1, G1, SH2, SC2, G2 = (i * DC for i in range(6))
MINUS = -3.0e38

B_ADA = 0
CONV = B_ADA + DEPTH * 6 * DC
PSC = CONV + DEPTH * CB * CONV_W
COND = PSC + DEPTH * CB
SMALL = COND + DC * NC9
O_CP = 0
O_PP = O_CP + CB * 2
O_CS = O_PP + CB * HIST
O_PS = O_CS + CB * NS * 2
ST_OUT = O_PS + CB * NS * HIST

PARTS = ((SH1, G1), (G1, SH2), (SH2, G2), (G2, 6 * DC))
FRONTS = 2 * DEPTH
W_STEPS = {"in": 2 * D // BW, "out": D // BW, "q": 2 * D // BW}
ADA_BLOCKS = 6 * D // BW


def stage_chunks(s):
    return TILE_CHUNKS + (SAMPLE_CHUNKS if s % 2 else 0)


def first_chunk(s):
    return sum(stage_chunks(i) for i in range(s))


def halves(name, f, n, samples):
    if samples:
        return [(name, f, (i, j)) for i in range(n) for j in range(2)]
    out = [(name, f, (0, 0))]
    for i in range(n):
        if i + 1 < n:
            out.append((name, f, (i + 1, 0)))
        out.append((name, f, (i, 1)))
    return out


def front_steps(f):
    smp = f % 2
    per = W_STEPS["q"] // (HEADS // PG)
    q = halves("q", f, W_STEPS["q"], smp)
    steps = [("stats_in", f, 0), ("turn_in", f, 0), ("samples_in", f, 0)] + halves("in", f, W_STEPS["in"], smp)
    steps += [("conv", f, 0), ("pool", f, 0)] + halves("out", f, W_STEPS["out"], smp)
    steps += [("gate_samples", f, 0), ("to_tokens", f, 0), ("norm1", f, 0), ("norm2", f, 0), ("turn_mid", f, 0),
              ("samples_mid", f, 0), ("to_h2", f, 0)]
    for i in range(HEADS // PG):
        last = q.index(("q", f, ((i + 1) * per - 1, 1)))
        steps += q[:last + 1] + [("scores", f, i), ("keys", f, i), ("pairs", f, i), ("decode", f, i), ("exps", f, i),
                                 ("gates", f, i)]
        q = q[last + 1:]
    if smp:
        steps += [(name, f, HEADS // PG) for name in ("keys", "pairs", "decode", "exps", "gates")]
    return steps


def ada_steps(layer):
    steps = []
    for step in halves("ada", layer, ADA_BLOCKS, False):
        steps.append(step)
        steps += [("bias", layer, k) for k, (_, hi) in enumerate(PARTS) if step[2] == (hi * P // BW - 1, 1)]
    return steps


def prologue_and_rest():
    front = front_steps(0)
    ada = [ada_steps(0), ada_steps(1)]
    n_in = sum(step[0] == "in" for step in front)
    n_out = sum(step[0] == "out" for step in front)

    def upto(part):
        taken = []
        while ("bias", 0, part) in ada[0]:
            taken.append(ada[0].pop(0))
        return taken

    steps = upto(0)
    gate1, counts = upto(1), {"in": 0, "out": 0}
    second = upto(2)
    while front:
        step = front.pop(0)
        steps.append(step)
        name = step[0]
        if name in counts:
            counts[name] += 1
        if name == "in":
            k = counts[name]
            steps += gate1[len(gate1) * (k - 1) // n_in:len(gate1) * k // n_in]
        elif name == "conv":
            steps += second[:4]
            second = second[4:]
        elif name == "out":
            k = n_out - counts[name]
            take = len(second) // (k + 1)
            steps += second[:take]
            second = second[take:]
        elif name in ("norm1", "norm2"):
            steps += upto(3) if name == "norm1" else []
            steps += ada[1][:4]
            del ada[1][:4]
        elif name == "scores":
            steps += ada[1][:8]
            del ada[1][:8]
        elif name == "gates":
            break
    return steps, front, ada[1]


def prologue():
    return prologue_and_rest()[0]


def steps_within(s):
    steps = front_steps(s + 1) if s + 1 < FRONTS else []
    if s == 0:
        _, front, ada = prologue_and_rest()
        steps = front + steps + ada
    return steps


ROOM = {"in": 1.0, "out": 1.0, "q": 1.0, "stats_in": 1.5, "turn_in": 1.0, "samples_in": 0.5, "conv": 2.0, "pool": 1.0,
        "gate_samples": 0.2, "to_tokens": 1.0, "norm1": 2.5, "norm2": 2.5, "turn_mid": 1.5, "samples_mid": 0.7,
        "to_h2": 1.5, "scores": 0.8, "keys": 1.2, "pairs": 0.9, "decode": 0.9,
        "exps": 0.1, "gates": 0.3, "ada": 0.35, "bias": 0.3}
SPAN = TILE_CHUNKS - 3


def plan(s):
    steps = steps_within(s)
    total = sum(ROOM[step[0]] for step in steps)
    out, done = [], 0.0
    for step in steps:
        out.append((int(1 + done / total * SPAN), step))
        done += ROOM[step[0]]
    return out


def blocks_of(steps):
    out = []
    for name, f, i in steps:
        if name in W_STEPS or name == "ada":
            if i[1] == 0:
                out.append((name, f, i[0]))
        elif name == "pool":
            out.append(("pool", f, 0))
        elif name == "norm1":
            out.append(("ln1", f, 0))
        elif name == "scores":
            out.append(("keys", f, i))
    return out


def weight_blocks():
    order = blocks_of(prologue())
    for s in range(FRONTS):
        order += blocks_of(steps_within(s)) + [("ln2", s, 0)]
    return order


def build_trunk(nc, x, xs, small, w_ada, w_in, w_out, w_q, keys, pool_w, ln1, ln2, conv_st, pool_st, uv,
                y, ys, st_new, bounce):
    BLOCKS = weight_blocks()
    AT = {b: n for n, b in enumerate(BLOCKS)}

    ctx = ExitStack()
    with ctx:
        def sb(name, shape, dt=F32):
            return ctx.enter_context(nc.sbuf_tensor(name, shape, dt))

        def sem(name):
            return ctx.enter_context(nc.semaphore(name))

        ring = sb("ring", [P, RC * KPC, SLOT])
        wring = sb("wring", [P, WSLOTS, BK])
        X = [sb(f"X{g}", [P, D]) for g in range(2)]
        Xs = sb("Xs", [NS, D])
        h2 = [sb(f"h2_{g}", [P, D]) for g in range(2)]
        h2rep = sb("h2rep", [P, D])
        hT = sb("hT", [P, DC, NMAX])
        zT = sb("zT", [P, ZB, NMAX])
        catT = sb("catT", [P, DC, NMAX])
        big0 = sb("big0", [P, CB * (2 * P + HIST)])
        big1 = sb("big1", [P, D])
        uext = sb("uext", [P, CB, 2 + P])
        pext = sb("pext", [P, CB, HIST + P])
        cs = sb("cs", [P, CB, NS, CONV_W])
        ps = sb("ps", [P, CB, NS, HIST + 1])
        sts = sb("sts", [P, ST_OUT])
        mod = [sb(f"mod{l}", [P, 6 * DC, NC9]) for l in range(DEPTH)]
        sm = sb("sm", [P, SMALL])
        csil = sb("csil", [P, DC, 32])
        rows = sb("rows", [P, 2, BW])
        mrows = sb("mrows", [P, 2, BW])
        diag = sb("diag", [P, RC, KPC, P])
        act_in = sb("act_in", [P, RC, KPC])
        act_out = sb("act_out", [P, RC, KPC])
        coef = sb("coef", [P, RC, KPC])
        ixs = sb("ixs", [P, RC, KPC], U32)
        idx = [sb(f"idx{g}", [P, HEADS * TOPK], U32) for g in range(2)]
        gates = [sb(f"gates{g}", [P, HEADS * TOPK]) for g in range(2)]
        s_pack = sb("s_pack", [P, 2, TOPK, 2], U32)
        s_ig = sb("s_ig", [P, 4, 2, 2], U32)
        kv = sb("kv", [P, 2 * PG, TOPK])
        ki = sb("ki", [P, 2 * PG, TOPK], U32)
        kf = sb("kf", [P, 2 * PG, TOPK])
        ev = sb("ev", [P, PG, TOPK])
        ei = sb("ei", [P, PG, TOPK], U32)
        ea = sb("ea", [P, PG, TOPK], U32)
        fa = sb("fa", [P, PG, TOPK])
        fb = sb("fb", [P, PG, TOPK])
        e1 = sb("e1", [P, PG * TOPK])
        e2 = sb("e2", [P, PG * TOPK])
        rs = sb("rs", [P, PG])
        hs = sb("hs", [P, DC, NS])
        bn = sb("bn", [P, 2, 6])
        mv = sb("mv", [P, 2])
        ve = sb("ve", [P, 1])
        sd = sb("sd", [P, 1])
        rstd = sb("rstd", [P, 1])
        ident = sb("ident", [P, P])
        iota = sb("iota", [P, TOPK])
        mask = sb("mask", [P, NS])
        pick9 = sb("pick9", [P, NC9])
        inv = sb("inv", [P, CB, TOPK])

        tok = catT[:, :, :].rearrange("p a b -> p (a b)")[:, 0:D]
        toks = h2rep[0:NS, :]
        xns = big1[0:NS, 0:D]
        g2s = big1[0:NS, 0:D]
        hsrep = big0[:, 0:D].rearrange("p (c t) -> p c t", c=DC)

        acc = ctx.enter_context(nc.psum_tensor("acc", [P, D], F32))
        scores = [ctx.enter_context(nc.psum_tensor(f"scores{i}", [P, 2 * PG, N_KEYS], F32)) for i in range(2)]
        s_scores = ctx.enter_context(nc.psum_tensor("s_scores", [P, 2 * PG, N_KEYS], F32))
        work = [ctx.enter_context(nc.psum_tensor(f"work{i}", [P, 512], F32)) for i in range(WORKS)]

        consts_in = sem("consts_in")
        state_in = sem("state_in")
        w_landed = [sem(f"w_landed{i}") for i in range(WSLOTS)]
        w_used = [sem(f"w_used{i}") for i in range(WSLOTS)]
        made = sem("made")
        work_full = sem("work_full")
        work_free = sem("work_free")
        dve_done = sem("dve_done")
        silu_done = sem("silu_done")
        mod_raw = sem("mod_raw")
        mod_ready = sem("mod_ready")
        var_ready = sem("var_ready")
        std_ready = sem("std_ready")
        xn_ready = sem("xn_ready")
        hT_ready = sem("hT_ready")
        hs_raw = sem("hs_raw")
        hs_ready = sem("hs_ready")
        z_ready = sem("z_ready")
        pooled_ready = sem("pooled_ready")
        cat_ready = sem("cat_ready")
        mT_ready = sem("mT_ready")
        ms_ready = sem("ms_ready")
        tok_ready = sem("tok_ready")
        h2_ready = sem("h2_ready")
        rep_ready = sem("rep_ready")
        q_ready = sem("q_ready")
        scores_ready = sem("scores_ready")
        scores_free = sem("scores_free")
        s_scores_ready = sem("s_scores_ready")
        s_scores_free = sem("s_scores_free")
        exp_in = sem("exp_in")
        exp_done = sem("exp_done")
        picks_ready = sem("picks_ready")
        pack_ready = sem("pack_ready")
        pack_out = sem("pack_out")
        spread = sem("spread")
        states_made = sem("states_made")
        ix_staged = sem("ix_staged")
        gathers_go = sem("gathers_go")
        uv_landed = [sem(f"uv_landed{i}") for i in range(RC)]
        acts_ready = sem("acts_ready")
        gelu_done = sem("gelu_done")
        coef_done = sem("coef_done")
        diag_ready = sem("diag_ready")
        chunk_used = sem("chunk_used")
        acc_free = sem("acc_free")
        g2_ready = sem("g2_ready")
        x_ready = sem("x_ready")
        stored = sem("stored")

        def wslot(n):
            return wring[:, n % WSLOTS, :]

        def arrived(eng, n):
            eng.wait_ge(w_landed[n % WSLOTS], 16 * (n // WSLOTS + 1))
            return wslot(n)

        def over_chunks(eng, s, lo, hi, body):
            def place(c):
                return (first_chunk(s) + c) % RC, (first_chunk(s) + c) // RC + 1

            g = lo
            while g < hi and place(g)[0]:
                body(g, *place(g))
                g += 1
            turns = (hi - g) // RC
            if turns > 1:
                with eng.Fori(0, turns) as t:
                    for r in range(RC):
                        body(t * RC + (g + r), r, t + place(g)[1])
                g += turns * RC
            while g < hi:
                body(g, *place(g))
                g += 1

        def run_stage(eng, s, first, body, last, steps, gate2, later=0):
            over_chunks(eng, s, 0, 1, first)
            at = 1
            for after, (name, f, i) in plan(s):
                to = max(at, min(after + later, TILE_CHUNKS - 1))
                over_chunks(eng, s, at, to, body)
                at = to
                steps[name](f, i)
            over_chunks(eng, s, at, TILE_CHUNKS - 1, body)
            gate2(s, P)
            over_chunks(eng, s, TILE_CHUNKS - 1, TILE_CHUNKS, last)

        def nothing(f, i):
            pass

        every_step = dict.fromkeys(ROOM, nothing)

        block = ctx.enter_context(nc.Block())

        @block.sync
        def _(sp):
            sp.dma_start(sm[:, :], small).then_inc(consts_in, 16)
            sp.dma_start(X[0][:, :], x[0:P, :]).then_inc(consts_in, 16)
            sp.dma_start(X[1][:, :], x[P:2 * P, :]).then_inc(consts_in, 16)
            sp.dma_start(Xs[:, :], xs).then_inc(consts_in, 16)
            stores = 0

            def load(n):
                kind, f, i = BLOCKS[n]
                layer = f if kind == "ada" else f // 2
                src = {"ada": w_ada, "in": w_in, "out": w_out, "q": w_q}.get(kind)
                if n >= WSLOTS:
                    sp.wait_ge(w_used[n % WSLOTS], n // WSLOTS)
                dst = wslot(n)
                if src is not None:
                    src = src[layer, i]
                elif kind == "keys":
                    dst, src = dst[:, 0:2 * PG * N_KEYS], keys[layer, i]
                elif kind == "pool":
                    dst, src = dst[:, 0:CB * P], pool_w[layer]
                else:
                    src = (ln1 if kind == "ln1" else ln2)[layer:layer + 1, :].broadcast_to([P, 2 * D])
                sp.dma_start(dst, src).then_inc(w_landed[n % WSLOTS], 16)

            n = 0
            for f in range(FRONTS):
                layer = f // 2
                if f % 2 == 1:
                    if layer:
                        sp.wait_ge(states_made, layer)
                    sp.dma_start(cs[:, :, :, :], conv_st[layer]).then_inc(state_in, 16)
                    sp.dma_start(ps[:, :, :, :], pool_st[layer]).then_inc(state_in, 16)
                while BLOCKS[n] != ("q", f, 1):
                    load(n)
                    n += 1
                if f % 2 == 1:
                    sp.wait_ge(states_made, layer + 1)
                    sp.dma_start(st_new[layer], sts[:, :]).then_inc(stored, 16)
                    stores += 1
            while n < len(BLOCKS):
                load(n)
                n += 1
            sp.wait_ge(x_ready, 1)
            sp.dma_start(y[0:P, :], X[0][:, :]).then_inc(stored, 16)
            sp.wait_ge(x_ready, 2)
            sp.dma_start(y[P:2 * P, :], X[1][:, :]).then_inc(stored, 16)
            sp.wait_ge(x_ready, 3)
            sp.dma_start(ys, Xs[:, :]).then_inc(stored, 16)
            sp.wait_ge(stored, 16 * (stores + 3))

        @block.gpsimd
        def _(pool):
            n_made = 0

            def make(ins):
                nonlocal n_made
                n_made += 1
                ins.then_inc(made, 1)
                pool.wait_ge(made, n_made)

            make(nc.gpsimd.memset(ident[:, :], 0.0))
            make(nc.gpsimd.affine_select(out=ident[:, :], in_=ident[:, :], compare_op=ALU.not_equal, fill=1.0,
                                         base=0, pattern=[[-1, P]], channel_multiplier=1))
            make(nc.gpsimd.iota(iota[:, :], [[1, TOPK]], base=0, channel_multiplier=0,
                                allow_small_or_imprecise_dtypes=True))
            make(nc.gpsimd.memset(mask[:, :], 1.0))
            make(nc.gpsimd.affine_select(out=mask[:, :], in_=mask[:, :], compare_op=ALU.is_ge, fill=0.0,
                                         base=0, pattern=[[-TOPK, NS]], channel_multiplier=1))
            make(nc.gpsimd.affine_select(out=mask[:, :], in_=mask[:, :], compare_op=ALU.is_ge, fill=0.0,
                                         base=TOPK - 1, pattern=[[TOPK, NS]], channel_multiplier=-1))
            make(nc.gpsimd.memset(csil[:, :, :], 0.0))
            make(nc.gpsimd.memset(pick9[:, :], 0.0))
            for q in range(4):
                make(nc.gpsimd.affine_select(out=pick9[:, :], in_=pick9[:, :], compare_op=ALU.not_equal, fill=1.0,
                                             base=-32 * q, pattern=[[-1, NC9]], channel_multiplier=1))
            for b, w in enumerate(WINDOWS):
                make(nc.gpsimd.memset(inv[:, b, :], 1.0 / w))
            for t in range(HIST):
                b = min(b for b, w in enumerate(WINDOWS) if w > t + 1)
                make(nc.gpsimd.memset(inv[:, b:CB, t:t + 1], 1.0 / (t + 1)))

            def gather(s, rows):
                G0 = first_chunk(s)

                def body(c, r, n):
                    if not isinstance(c, int) or G0 + c >= RC:
                        pool.wait_ge(chunk_used, c + (G0 - RC + 1))
                    out, src = rows(c, ixs[:, r, :])
                    nc.gpsimd.tensor_copy(out, src).then_inc(ix_staged, 1)
                    pool.wait_ge(ix_staged, c + (G0 + 1))
                    pool.sem_inc(gathers_go, 1)
                    for j in range(KPC):
                        nc.gpsimd.indirect_dma_start(ring[:, r * KPC + j, :], None, uv,
                                                     bass.IndirectOffsetOnAxis(ixs[:, r, j:j + 1], 0))\
                            .then_inc(uv_landed[r], 16)
                return body

            for s in range(FRONTS):
                body = gather(s, lambda c, to, g=s % 2: (to, idx[g][:, bass.ds(c * KPC, KPC)]))
                per = TILE_CHUNKS // (HEADS // PG)
                for i in range(HEADS // PG):
                    pool.wait_ge(picks_ready, s * (HEADS // PG) + i + 1)
                    lo = i * per
                    if s == 0 and i == 0:
                        over_chunks(pool, s, 0, RC, body)
                        lo = RC
                    over_chunks(pool, s, lo, (i + 1) * per, body)
                if s % 2:
                    pool.wait_ge(spread, 16 * (s // 2 + 1))
                    for c in range(TILE_CHUNKS, TILE_CHUNKS + SAMPLE_CHUNKS):
                        q = (c - TILE_CHUNKS) * KPC // 2
                        body = gather(s, lambda c, to, q=q: (to.rearrange("p (q g) -> p q g", g=2),
                                                             s_ig[:, q:q + KPC // 2, 0, :]))
                        over_chunks(pool, s, c, c + 1, body)

        @block.scalar
        def _(act):
            item = [0]

            def drain(*copies, block=None):
                act.wait_ge(work_full, item[0] + 1)
                if block is not None:
                    act.sem_inc(w_used[AT[block] % WSLOTS], 1)
                bank = work[item[0] % WORKS]
                for out, pick, scale, bias in copies:
                    last = nc.scalar.activation(out, pick(bank), ACT.Identity, bias=bias, scale=scale)
                last.then_inc(work_free, 1)
                item[0] += 1

            def after_drain(sig):
                act.wait_ge(work_free, item[0])
                act.sem_inc(sig, 1)

            def cols(lo, hi, parts=P):
                return lambda bank: bank[0:parts, lo:hi]

            def root(parts=P, n=[0]):
                n[0] += 1
                act.wait_ge(var_ready, n[0])
                nc.scalar.activation(sd[0:parts, :], ve[0:parts, :], ACT.Sqrt).then_inc(std_ready, 1)

            def transposed(f, shift, scale):
                m = mod[f // 2]
                act.wait_ge(mod_ready, len(PARTS) * (f // 2) + (1 if shift == SH1 else 3))
                for half in range(2):
                    drain(*[(hT[:, half * 4 + c, 0:P], cols(c * P, (c + 1) * P),
                             m[:, scale + half * 4 + c, 0:1], m[:, shift + half * 4 + c, 0:1])
                            for c in range(4)])
                after_drain(hT_ready)
                if f % 2:
                    drain((hs[:, :, :].rearrange("p a b -> p (a b)"), cols(0, DC * NS), 1.0, 0.0))
                    after_drain(hs_raw)

            def stats_in(f, _):
                root()
                if f % 2:
                    root(NS)

            def projected(name, out, gate=None, sig=None, each=False):
                def step(f, at):
                    i, half = at
                    block = (name, f, i)
                    if gate is not None:
                        act.wait_ge(mod_ready, len(PARTS) * (f // 2) + 2)

                    def g(c):
                        return 1.0 if gate is None else mod[f // 2][:, gate + c, 0:1]

                    if f % 2:
                        c = 2 * i + half
                        copies = [(out[:, c, 0:P], cols(0, P), g(c), 0.0), (out[:, c, P:NMAX], cols(P, NMAX), 1.0, 0.0)]
                        if gate is None:
                            copies = [(out[:, c, :], cols(0, NMAX), 1.0, 0.0)]
                        drain(*copies, block=block if half else None)
                    elif half == 0:
                        drain((rows[:, i % 2, :], cols(0, BW), 1.0, 0.0), block=block)
                    else:
                        drain(*[(out[:, 2 * i + j, 0:P], cols(j * P, (j + 1) * P), g(2 * i + j), 0.0) for j in range(2)])
                    if half and (each or i == W_STEPS[name] - 1):
                        after_drain(sig)
                return step

            def pool(f, _):
                l = f // 2
                n = P + NS * (f % 2)
                for g in range(CB):
                    drain((catT[:, CB + g, 0:n], cols(0, n), sm[:, PSC + l * CB + g:PSC + l * CB + g + 1], 0.0),
                          block=("pool", f, 0) if g == CB - 1 else None)
                after_drain(cat_ready)

            def by_halves(out, parts=P):
                for half in range(2):
                    drain((out[:, half * 512:(half + 1) * 512], cols(0, 512, parts), 1.0, 0.0))

            def to_tokens(f, _):
                by_halves(tok)
                if f % 2:
                    by_halves(toks, NS)
                after_drain(tok_ready)

            def norm2(f, _):
                root()
                if f % 2:
                    root(NS)

            def to_h2(f, _):
                by_halves(h2[f % 2])
                if f % 2:
                    by_halves(h2rep)
                after_drain(h2_ready)

            n_exp = [0]

            def exps(f, i):
                n_exp[0] += 1
                act.wait_ge(exp_in, n_exp[0])
                nc.scalar.activation(kv[:, 0:PG, :], kv[:, 0:PG, :], ACT.Exp).then_inc(exp_done, 1)

            def spread_samples(f, i):
                if i < HEADS // PG:
                    return
                act.wait_ge(pack_ready, f // 2 + 1)
                for q in range(4):
                    act.dma_start(bounce[q].rearrange("a t x -> t a x"),
                                  s_pack[32 * q:32 * q + NS, :, :, :].rearrange("p a k g -> p a (k g)"))\
                        .then_inc(pack_out, 16)
                act.wait_ge(pack_out, 64 * (f // 2 + 1))
                act.dma_start(s_ig[:, :, :, :].rearrange("p q a g -> p (q a) g"),
                              bounce.rearrange("q a t (k g) -> (t k) (q a) g", g=2)).then_inc(spread, 16)

            def ada(layer, at):
                i, half = at
                if half == 0:
                    drain((mrows[:, i % 2, :], cols(0, BW), 1.0, 0.0), block=("ada", layer, i))
                else:
                    drain((mod[layer][:, 2 * i:2 * i + 2, :].rearrange("p a b -> p (a b)"), cols(0, 2 * NC9), 1.0, 0.0))
                    if any(2 * i + 2 == hi for _, hi in PARTS):
                        after_drain(mod_raw)

            steps = every_step | {
                "stats_in": stats_in, "turn_in": lambda f, i: transposed(f, SH1, SC1),
                "in": projected("in", zT, sig=z_ready), "pool": pool, "out": projected("out", hT, gate=G1, sig=mT_ready),
                "to_tokens": to_tokens, "norm1": stats_in, "norm2": norm2,
                "turn_mid": lambda f, i: transposed(f, SH2, SC2), "to_h2": to_h2,
                "q": projected("q", zT, sig=q_ready, each=True), "exps": exps, "gates": spread_samples, "ada": ada}

            def weigh(s, gate_of, base, width):
                G0 = first_chunk(s)

                def body(c, r, n):
                    act.wait_ge(acts_ready, c + (G0 + 1))
                    nc.scalar.activation(act_out[:, r, :], act_in[:, r, :], ACT.Gelu).then_inc(gelu_done, 1)
                    act.wait_ge(gelu_done, c + (G0 + 1))
                    for j in range(KPC):
                        last = nc.scalar.activation(coef[:, r, j:j + 1], act_out[:, r, j:j + 1], ACT.Copy, scale=gate_of(c, j))
                    last.then_inc(coef_done, 1)
                    act.wait_ge(coef_done, c + (G0 + 1))
                    for j in range(KPC):
                        last = nc.scalar.activation(diag[:, r, j, 0:width], base[:, 0:width], ACT.Copy, scale=coef[:, r, j:j + 1])
                    last.then_inc(diag_ready, 1)
                return body

            def gate2(f, parts):
                by_halves(tok if parts == P else g2s, parts)
                after_drain(g2_ready)

            act.wait_ge(consts_in, 16 * 4)
            act.wait_ge(made, 7)
            nc.scalar.activation(csil[:, :, 0:NC9], sm[:, COND:SMALL].rearrange("p (k r) -> p k r", k=DC),
                                 ACT.Silu).then_inc(silu_done, 1)
            for name, f, i in prologue():
                steps[name](f, i)
            for s in range(FRONTS):
                body = weigh(s, lambda c, j, g=s % 2: gates[g][:, bass.ds(c * KPC + j, 1)], ident, P)
                run_stage(act, s, body, body, body, steps, gate2, later=1)
                root()
                if s % 2:
                    def sample_gate(c, j):
                        at = (c - TILE_CHUNKS) * KPC + j
                        return s_ig[:, at // 2, 1, at % 2:at % 2 + 1].bitcast(F32)

                    act.wait_ge(spread, 16 * (s // 2 + 1))
                    body = weigh(s, sample_gate, mask, NS)
                    over_chunks(act, s, TILE_CHUNKS, stage_chunks(s) - 1, body)
                    gate2(s, NS)
                    over_chunks(act, s, stage_chunks(s) - 1, stage_chunks(s), body)
                    root(NS)

        @block.vector
        def _(dve):
            counts = {}

            def link(ins, sig=dve_done):
                counts[id(sig)] = counts.get(id(sig), 0) + 1
                ins.then_inc(sig, 1)
                dve.wait_ge(sig, counts[id(sig)])

            roots = [0]

            def normalise(src, out, parts=P, sig=dve_done):
                for i in range(2):
                    last = nc.vector.bn_stats(bn[0:parts, i, :], src[:, i * 512:(i + 1) * 512])
                link(last)
                link(nc.vector.bn_aggr(mv[0:parts, :], bn[0:parts, :, :].rearrange("p a b -> p (a b)")))
                nc.vector.tensor_scalar(ve[0:parts, :], mv[0:parts, 1:2], EPS, None, ALU.add).then_inc(var_ready, 1)
                roots[0] += 1
                dve.wait_ge(std_ready, roots[0])
                link(nc.vector.reciprocal(rstd[0:parts, :], sd[0:parts, :]))
                link(nc.vector.tensor_scalar(out, src, mv[0:parts, 0:1], rstd[0:parts, 0:1], ALU.subtract, ALU.mult),
                     sig)

            def gain(t, n, parts=P):
                gb = arrived(dve, n)
                link(nc.vector.tensor_tensor(t, t, gb[0:parts, 0:D], ALU.mult))
                return nc.vector.tensor_tensor(t, t, gb[0:parts, D:2 * D], ALU.add)

            def modulate_samples(f, shift, scale):
                m = mod[f // 2]
                link(nc.vector.tensor_tensor(hs[:, :, :], hs[:, :, :], m[:, scale:scale + DC, 1:NC9], ALU.mult))
                link(nc.vector.tensor_tensor(hT[:, :, P:NMAX], hs[:, :, :], m[:, shift:shift + DC, 1:NC9], ALU.add),
                     hs_ready)

            def stats_in(f, _):
                normalise(X[f % 2][:, :], h2[f % 2][:, :], P, xn_ready)
                if f % 2:
                    normalise(Xs[:, :], xns, NS, xn_ready)

            def samples_in(f, _):
                if f % 2:
                    dve.wait_ge(hs_raw, f // 2 * 2 + 1)
                    modulate_samples(f, SH1, SC1)

            def conv_weight(l, b, k):
                at = CONV + (l * CB + b) * CONV_W + k
                return sm[:, at:at + 1]

            def conv(f, _):
                l, smp = f // 2, f % 2
                if f % 2 == 0:
                    nc.vector.memset(uext[:, :, 0:2], 0.0)
                    link(nc.vector.memset(pext[:, :, 0:HIST], 0.0))
                else:
                    nc.vector.tensor_copy(uext[:, :, 0:2], uext[:, :, P:P + 2])
                    link(nc.vector.tensor_copy(pext[:, :, 0:HIST], pext[:, :, P:P + HIST]))
                dve.wait_ge(z_ready, f + 1)
                nc.vector.tensor_tensor(uext[:, :, 2:2 + P], zT[:, CB:2 * CB, 0:P], zT[:, 2 * CB:3 * CB, 0:P], ALU.mult)
                link(nc.vector.tensor_copy(pext[:, :, HIST:HIST + P], zT[:, 3 * CB:ZB, 0:P]))
                yT = big0[:, 0:CB * P].rearrange("p (b t) -> p b t", b=CB)
                s0 = big1[:, 0:CB * (HIST + P)].rearrange("p (b t) -> p b t", b=CB)
                s1 = big0[:, CB * P:CB * P + CB * (HIST + P)].rearrange("p (b t) -> p b t", b=CB)
                E = HIST + P
                for b in range(CB):
                    nc.vector.tensor_scalar(yT[:, b, :], uext[:, b, 0:P], conv_weight(l, b, 0), None, ALU.mult)
                link(nc.vector.tensor_tensor(s0[:, :, 1:E], pext[:, :, 1:E], pext[:, :, 0:E - 1], ALU.add))
                for b in range(CB):
                    nc.vector.scalar_tensor_tensor(yT[:, b, :], uext[:, b, 1:1 + P], conv_weight(l, b, 1),
                                                   yT[:, b, :], ALU.mult, ALU.add)
                link(nc.vector.tensor_tensor(s1[:, 1:CB, 3:E], s0[:, 1:CB, 3:E], s0[:, 1:CB, 1:E - 2], ALU.add))
                for b in range(CB):
                    nc.vector.scalar_tensor_tensor(yT[:, b, :], uext[:, b, 2:2 + P], conv_weight(l, b, 2),
                                                   yT[:, b, :], ALU.mult, ALU.add)
                link(nc.vector.tensor_tensor(s0[:, 2:CB, 7:E], s1[:, 2:CB, 7:E], s1[:, 2:CB, 3:E - 4], ALU.add))
                nc.vector.tensor_tensor(catT[:, 0:CB, 0:P], zT[:, 0:CB, 0:P], yT, ALU.mult)
                link(nc.vector.tensor_tensor(s1[:, 3:CB, HIST:E], s0[:, 3:CB, HIST:E], s0[:, 3:CB, 7:E - 8], ALU.add))
                for b, w in enumerate(WINDOWS):
                    last = nc.vector.scalar_tensor_tensor(zT[:, 3 * CB + b, 0:P], (s0, s1)[b % 2][:, b, HIST:E], 1.0 / w,
                                                          pext[:, b, HIST:E], ALU.mult, ALU.subtract)
                if f % 2 == 0:
                    link(last)
                    for b in range(CB):
                        last = nc.vector.tensor_tensor(zT[:, 3 * CB + b, 0:TOPK], (s0, s1)[b % 2][:, b, HIST:HIST + TOPK],
                                                       inv[:, b, :], ALU.mult)
                    link(last)
                    last = nc.vector.tensor_tensor(zT[:, 3 * CB:ZB, 0:TOPK], zT[:, 3 * CB:ZB, 0:TOPK],
                                                   pext[:, :, HIST:HIST + TOPK], ALU.subtract)
                if smp:
                    link(last)
                    dve.wait_ge(state_in, 32 * (l + 1))
                    nc.vector.tensor_tensor(cs[:, :, :, 2:3].rearrange("p b t o -> p b (t o)"),
                                            zT[:, CB:2 * CB, P:NMAX], zT[:, 2 * CB:3 * CB, P:NMAX], ALU.mult)
                    link(nc.vector.tensor_copy(ps[:, :, :, HIST:HIST + 1].rearrange("p b t o -> p b (t o)"),
                                               zT[:, 3 * CB:ZB, P:NMAX]))
                    ysT = big0[:, 0:CB * NS].rearrange("p (b t) -> p b t", b=CB)
                    sw = big0[:, CB * NS:2 * CB * NS].rearrange("p (b t) -> p b t", b=CB)
                    for b, w in enumerate(WINDOWS):
                        nc.vector.tensor_scalar(ysT[:, b, :], cs[:, b, :, 0], conv_weight(l, b, 0), None, ALU.mult)
                        last = nc.vector.tensor_reduce(sw[:, b, :], ps[:, b, :, HIST + 1 - w:HIST + 1], AX.X, ALU.add)
                    link(last)
                    for k in (1, 2):
                        for b in range(CB):
                            last = nc.vector.scalar_tensor_tensor(ysT[:, b, :], cs[:, b, :, k], conv_weight(l, b, k),
                                                                  ysT[:, b, :], ALU.mult, ALU.add)
                        link(last)
                    for b, w in enumerate(WINDOWS):
                        nc.vector.scalar_tensor_tensor(zT[:, 3 * CB + b, P:NMAX], sw[:, b, :], 1.0 / w, ps[:, b, :, HIST],
                                                       ALU.mult, ALU.subtract)
                    last = nc.vector.tensor_tensor(catT[:, 0:CB, P:NMAX], zT[:, 0:CB, P:NMAX], ysT, ALU.mult)
                link(last, pooled_ready)
                if smp:
                    if l:
                        dve.wait_ge(stored, 16 * l)
                    nc.vector.tensor_copy(sts[:, O_CP:O_PP].rearrange("p (b k) -> p b k", b=CB), uext[:, :, P:P + 2])
                    nc.vector.tensor_copy(sts[:, O_PP:O_CS].rearrange("p (b k) -> p b k", b=CB), pext[:, :, P:P + HIST])
                    nc.vector.tensor_copy(sts[:, O_CS:O_PS].rearrange("p (b t k) -> p (b t) k", b=CB, t=NS),
                                          cs[:, :, :, 1:3].rearrange("p b t k -> p (b t) k"))
                    nc.vector.tensor_copy(sts[:, O_PS:ST_OUT].rearrange("p (b t k) -> p (b t) k", b=CB, t=NS),
                                          ps[:, :, :, 1:HIST + 1].rearrange("p b t k -> p (b t) k"))\
                        .then_inc(states_made, 1)

            def gate_samples(f, _):
                if f % 2:
                    dve.wait_ge(mT_ready, f + 1)
                    link(nc.vector.tensor_tensor(hT[:, :, P:NMAX], hT[:, :, P:NMAX], mod[f // 2][:, G1:G1 + DC, 1:NC9],
                                                 ALU.mult), ms_ready)

            def norm1(f, _):
                n = AT["ln1", f, 0]
                dve.wait_ge(tok_ready, f + 1)
                sets = [(X[f % 2][:, :], tok, P)] + ([(Xs[:, :], toks, NS)] if f % 2 else [])
                for xt, t, parts in sets:
                    link(nc.vector.scalar_tensor_tensor(xt, xt, ALPHA, t, ALU.mult, ALU.add))
                    normalise(xt, xt, parts)
                    last = gain(xt, n, parts)
                    if parts == P and f % 2:
                        link(last)
                last.then_inc(w_used[n % WSLOTS], 1)
                dve.wait_ge(w_used[n % WSLOTS], n // WSLOTS + 1)

            def samples_mid(f, _):
                if f % 2:
                    dve.wait_ge(hs_raw, f // 2 * 2 + 2)
                    modulate_samples(f, SH2, SC2)
                    for c in range(DC):
                        last = nc.vector.tensor_copy(hsrep[:, c, :].rearrange("p (t k) -> p t k", k=TOPK),
                                                     hT[:, c, P:NMAX].unsqueeze(2).broadcast_to([P, NS, TOPK]))
                    link(last, rep_ready)

            def search(src, tmp, values, places, free=None):
                n = src.shape[1]
                for i in range(n):
                    last = nc.vector.max(values[:, i, 0:8], src[:, i, :])
                link(last)
                for i in range(n):
                    nc.vector.max_index(places[:, i, 0:8], values[:, i, 0:8], src[:, i, :])
                    last = nc.vector.match_replace(tmp[:, i, :], values[:, i, 0:8], src[:, i, :], MINUS)
                link(last, free or dve_done)
                for i in range(n):
                    last = nc.vector.max(values[:, i, 8:16], tmp[:, i, :])
                link(last)
                for i in range(n):
                    last = nc.vector.max_index(places[:, i, 8:16], values[:, i, 8:16], tmp[:, i, :])
                link(last)

            n_scores = [0]

            def search_keys(f, i):
                if i < HEADS // PG:
                    now, free = scores[n_scores[0] % 2], scores_free
                    n_scores[0] += 1
                    dve.wait_ge(scores_ready, n_scores[0])
                    dve.sem_inc(w_used[AT["keys", f, i] % WSLOTS], 1)
                else:
                    now, free = s_scores, s_scores_free
                    dve.wait_ge(s_scores_ready, f // 2 + 1)
                search(now, big0[:, 0:2 * PG * N_KEYS].rearrange("p (i k) -> p i k", k=N_KEYS), kv, ki, free)

            def search_pairs(f, i):
                nc.vector.tensor_copy(kf[:, :, :], ki[:, :, :])
                pairs = big1[:, 0:PG * 256].rearrange("p (h i j) -> p h i j", h=PG, i=TOPK)
                v4 = kv[:, :, :].rearrange("p (h s) k -> p h s k", s=2)
                one = v4[:, :, 0, :].unsqueeze(3).broadcast_to([P, PG, TOPK, TOPK])
                two = v4[:, :, 1, :].unsqueeze(2).broadcast_to([P, PG, TOPK, TOPK])
                link(nc.vector.tensor_tensor(pairs, one, two, ALU.add))
                tmp = big0[:, 0:PG * 256].rearrange("p (i k) -> p i k", k=256)
                search(big1[:, 0:PG * 256].rearrange("p (i k) -> p i k", k=256), tmp, ev, ei)

            def places(f, i):
                if i < HEADS // PG:
                    at = slice(i * PG * TOPK, (i + 1) * PG * TOPK)
                    return [t[f % 2][:, at].rearrange("p (h k) -> p h k", k=TOPK) for t in (idx, gates)]
                return (s_pack[:, 0, :, :].rearrange("p k h -> p h k"),
                        s_pack[:, 1, :, :].bitcast(F32).rearrange("p k h -> p h k"))

            n_exp = [0]

            def decode(f, i):
                l, nh = f // 2, PG
                number = places(f, i)[0]
                n = nh * TOPK
                ex = kv[:, 0:nh, :]
                link(nc.vector.tensor_tensor(ex, ev[:, 0:nh, :],
                                             ev[:, 0:nh, 0:1].broadcast_to([P, nh, TOPK]), ALU.subtract), exp_in)
                link(nc.vector.tensor_scalar(ea[:, 0:nh, :], ei[:, 0:nh, :], 4, None, ALU.logical_shift_right))
                link(nc.vector.tensor_copy(fa[:, 0:nh, :], ea[:, 0:nh, :]))
                link(nc.vector.tensor_scalar(ea[:, 0:nh, :], ei[:, 0:nh, :], TOPK - 1, None, ALU.bitwise_and))
                link(nc.vector.tensor_copy(fb[:, 0:nh, :], ea[:, 0:nh, :]))
                k4 = kf[:, 0:2 * nh, :].rearrange("p (h s) k -> p h s k", s=2)
                for place, half, hit, out in ((fa, 0, big0, e1), (fb, 1, big1, e2)):
                    h3 = hit[:, 0:n * TOPK].rearrange("p (a j) -> p a j", j=TOPK)
                    h4 = hit[:, 0:n * TOPK].rearrange("p (h a j) -> p h a j", h=nh, j=TOPK)
                    flat = place[:, 0:nh, :].rearrange("p h k -> p (h k)").unsqueeze(2).broadcast_to([P, n, TOPK])
                    link(nc.vector.tensor_tensor(h3, flat, iota[:, :].unsqueeze(1).broadcast_to([P, n, TOPK]), ALU.is_equal))
                    link(nc.vector.tensor_tensor(h4, h4, k4[:, :, half, :].unsqueeze(2).broadcast_to([P, nh, TOPK, TOPK]),
                                                 ALU.mult))
                    link(nc.vector.tensor_reduce(out[:, 0:n], h3, AX.X, ALU.add))
                link(nc.vector.scalar_tensor_tensor(e1[:, 0:n], e1[:, 0:n], float(N_KEYS), e2[:, 0:n], ALU.mult, ALU.add))
                if i == HEADS // PG and l:
                    dve.wait_ge(pack_out, 64 * l)
                nc.vector.tensor_scalar(number, e1[:, :].rearrange("p (h k) -> p h k", k=TOPK), float(l * N_EXPERTS),
                                        None, ALU.add)

            def soft_gates(f, i):
                ex = kv[:, 0:PG, :]
                n_exp[0] += 1
                dve.wait_ge(exp_done, n_exp[0])
                link(nc.vector.tensor_reduce(rs[:, :], ex, AX.X, ALU.add))
                link(nc.vector.reciprocal(rs[:, :], rs[:, :]))
                link(nc.vector.tensor_tensor(places(f, i)[1], ex, rs[:, :].unsqueeze(2).broadcast_to([P, PG, TOPK]),
                                             ALU.mult), picks_ready if i < HEADS // PG else pack_ready)

            def bias(layer, part):
                dve.wait_ge(mod_raw, len(PARTS) * layer + part + 1)
                m = mod[layer]
                lo, hi = PARTS[part]
                b = sm[:, B_ADA + layer * 6 * DC + lo:B_ADA + layer * 6 * DC + hi]
                scaled = part in (0, 2)
                link(nc.vector.tensor_tensor(m[:, lo:hi, :], m[:, lo:hi, :], b.unsqueeze(2).broadcast_to([P, hi - lo, NC9]),
                                             ALU.add), dve_done if scaled else mod_ready)
                if scaled:
                    sc = m[:, lo + DC:hi, :]
                    link(nc.vector.tensor_scalar(sc, sc, 1.0, None, ALU.add), mod_ready)

            steps = every_step | {
                "stats_in": stats_in, "samples_in": samples_in, "conv": conv, "gate_samples": gate_samples,
                "norm1": norm1, "norm2": stats_in, "samples_mid": samples_mid, "keys": search_keys,
                "pairs": search_pairs, "decode": decode, "gates": soft_gates, "bias": bias}

            def dots(xt, s):
                G0 = first_chunk(s)

                def body(c, r, n):
                    dve.wait_ge(uv_landed[r], n * (16 * KPC))
                    for j in range(KPC):
                        u = ring[:, r * KPC + j, 0:D]
                        last = nc.vector.scalar_tensor_tensor(u, u, 1.0, xt, ALU.mult, ALU.mult,
                                                              accum_out=act_in[:, r, j:j + 1])
                    last.then_inc(acts_ready, 1)
                return body

            gate2s = [0]

            def finish(s, parts):
                t = tok if parts == P else g2s
                xt = X[s % 2][:, :] if parts == P else Xs[:, :]
                n = AT["ln2", s, 0]
                gate2s[0] += 1
                dve.wait_ge(g2_ready, gate2s[0])
                done = first_chunk(s) + (TILE_CHUNKS if parts == P else stage_chunks(s))
                dve.wait_ge(chunk_used, done)
                link(nc.vector.tensor_tensor(t, t, acc[0:parts, :], ALU.mult), acc_free)
                link(nc.vector.scalar_tensor_tensor(xt, xt, ALPHA, t, ALU.mult, ALU.add))
                normalise(xt, xt, parts)
                last = gain(xt, n, parts)
                if s >= FRONTS - 2:
                    link(last, x_ready)
                    last = None
                if parts == NS or s % 2 == 0:
                    if last is None:
                        last = nc.vector.tensor_copy(ve[0:1, :], mv[0:1, 0:1])
                    last.then_inc(w_used[n % WSLOTS], 1)
                    dve.wait_ge(w_used[n % WSLOTS], n // WSLOTS + 1)
                elif last is not None:
                    link(last)

            link(nc.vector.memset(s_scores[:, :, :], 0.0), s_scores_free)
            dve.wait_ge(made, 12 + len(WINDOWS) + HIST)
            dve.wait_ge(consts_in, 16 * 4)
            for name, f, i in prologue():
                steps[name](f, i)
            for s in range(FRONTS):
                dve.wait_ge(h2_ready, s + 1)
                body = dots(h2[s % 2][:, :], s)
                run_stage(dve, s, body, body, body, steps, lambda s, parts: None, later=1)
                finish(s, P)
                if s % 2:
                    over_chunks(dve, s, TILE_CHUNKS, stage_chunks(s), dots(h2rep[:, :], s))
                    finish(s, NS)

        @block.tensor
        def _(pe):
            item = [0]

            def bank():
                if item[0] >= WORKS:
                    pe.wait_ge(work_free, item[0] - WORKS + 1)
                b = work[item[0] % WORKS]
                item[0] += 1
                return b

            def transposes(src, parts=P):
                for half in range(2):
                    b = bank()
                    for c in range(4):
                        last = nc.tensor.transpose(b[:, c * P:(c + 1) * P], src[:, (half * 4 + c) * P:(half * 4 + c + 1) * P],
                                                   ident[:, :])
                    last.then_inc(work_full, 1)

            def to_channels(f, nth):
                smp = f % 2
                done = sum(4 if g % 2 else 2 for g in range(f)) + nth * (2 if smp else 1)
                pe.wait_ge(xn_ready, done + 1)
                transposes(h2[f % 2])
                if smp:
                    pe.wait_ge(xn_ready, done + 2)
                    b = bank()
                    for c in range(DC):
                        last = nc.tensor.matmul(b[:, c * NS:(c + 1) * NS], xns[:, c * P:(c + 1) * P], ident[0:NS, 0:NS],
                                                start=True, stop=True)
                    last.then_inc(work_full, 1)

            def tile_to_tokens():
                for half in range(2):
                    b = bank()
                    for c in range(4):
                        last = nc.tensor.transpose(b[:, c * P:(c + 1) * P], hT[:, half * 4 + c, 0:P], ident[:, :])
                    last.then_inc(work_full, 1)

            def dense(name, rhs, wait):
                def step(f, at):
                    i, half = at
                    if half == 0:
                        wait(f)
                    nb = AT[name, f, i]
                    w = wslot(nb).rearrange("p (k c) -> p k c", k=DC)
                    if half == 0:
                        arrived(pe, nb)
                    if f % 2:
                        b = bank()
                        for k in range(DC):
                            last = nc.tensor.matmul(b[:, 0:NMAX], w[:, k, half * P:(half + 1) * P], rhs[:, k, :],
                                                    start=(k == 0), stop=(k == DC - 1))
                        last.then_inc(work_full, 1)
                    elif half == 0:
                        b = bank()
                        for k in range(DC):
                            last = nc.tensor.matmul(b[:, 0:BW], rhs[:, k, 0:P], w[:, k, :], start=(k == 0),
                                                    stop=(k == DC - 1))
                        last.then_inc(work_full, 1)
                        rows_item[name, f, i] = item[0]
                    else:
                        pe.wait_ge(work_free, rows_item[name, f, i])
                        b = bank()
                        for j in range(BW // P):
                            last = nc.tensor.transpose(b[:, j * P:(j + 1) * P], rows[:, i % 2, j * P:(j + 1) * P],
                                                       ident[:, :])
                        last.then_inc(work_full, 1)
                return step

            rows_item = {}

            def modulated(f):
                pe.wait_ge(hT_ready, 2 * f + 1)
                if f % 2:
                    pe.wait_ge(hs_ready, f // 2 * 2 + 1)

            def modulated_mid(f):
                pe.wait_ge(hT_ready, 2 * f + 2)
                if f % 2:
                    pe.wait_ge(hs_ready, f // 2 * 2 + 2)

            def pool(f, _):
                n = P + NS * (f % 2)
                pe.wait_ge(pooled_ready, f + 1)
                w = arrived(pe, AT["pool", f, 0])
                for g in range(CB):
                    b = bank()
                    nc.tensor.matmul(b[:, 0:n], w[:, g * P:(g + 1) * P], zT[:, 3 * CB + g, 0:n], start=True, stop=True)\
                        .then_inc(work_full, 1)

            def to_tokens(f, _):
                pe.wait_ge(mT_ready, f + 1)
                tile_to_tokens()
                if f % 2:
                    pe.wait_ge(ms_ready, f // 2 + 1)
                    for half in range(2):
                        b = bank()
                        for c in range(4):
                            last = nc.tensor.matmul(b[0:NS, c * P:(c + 1) * P], hT[:, half * 4 + c, P:NMAX], ident[:, :],
                                                    start=True, stop=True)
                        last.then_inc(work_full, 1)

            def to_h2(f, _):
                pe.wait_ge(hT_ready, 2 * f + 2)
                tile_to_tokens()
                if f % 2:
                    pe.wait_ge(rep_ready, f // 2 + 1)
                    for half in range(2):
                        b = bank()
                        for c in range(4):
                            last = nc.tensor.matmul(b[:, c * P:(c + 1) * P], hsrep[:, half * 4 + c, :], ident[:, :],
                                                    start=True, stop=True)
                        last.then_inc(work_full, 1)

            n_scores = [0]

            def scores_bank():
                if n_scores[0] >= 2:
                    pe.wait_ge(scores_free, n_scores[0] - 1)
                b = scores[n_scores[0] % 2]
                n_scores[0] += 1
                return b

            def score(f, i):
                per = W_STEPS["q"] // (HEADS // PG)
                pe.wait_ge(q_ready, f * W_STEPS["q"] + (i + 1) * per)
                k = arrived(pe, AT["keys", f, i])[:, 0:2 * PG * N_KEYS].rearrange("p (i c) -> p i c", c=N_KEYS)
                b = scores_bank()
                if f % 2:
                    if i == 0:
                        pe.wait_ge(s_scores_free, f // 2 + 1)
                    for hp in range(2 * PG):
                        head, half = PG * i + hp // 2, hp % 2
                        q = head % 4
                        last = nc.tensor.matmul(s_scores[32 * q:32 * q + NS, 2 * (head // 4) + half, :],
                                                zT[:, 2 * head + half, P:NMAX], k[:, hp, :], start=True, stop=True)
                    if i == HEADS // PG - 1:
                        last.then_inc(s_scores_ready, 1)
                for hp in range(2 * PG):
                    last = nc.tensor.matmul(b[:, hp, :], zT[:, 2 * PG * i + hp, 0:P], k[:, hp, :], start=True, stop=True)
                last.then_inc(scores_ready, 1)

            def ada(layer, at):
                i, half = at
                if half == 0:
                    w = arrived(pe, AT["ada", layer, i]).rearrange("p (k c) -> p k c", k=DC)
                    b = bank()
                    for k in range(DC):
                        strip = slice(32 * (k % 4), 32 * (k % 4) + 32)
                        last = nc.tensor.matmul(b[strip, 0:BW], csil[:, k, :], w[:, k, :], start=(k < 4), stop=(k >= 4))
                    last.then_inc(work_full, 1)
                    rows_item["ada", layer, i] = item[0]
                else:
                    pe.wait_ge(work_free, rows_item["ada", layer, i])
                    b = bank()
                    for j in range(BW // P):
                        last = nc.tensor.matmul(b[:, j * NC9:(j + 1) * NC9], mrows[:, i % 2, j * P:(j + 1) * P],
                                                pick9[:, :], start=True, stop=True)
                    last.then_inc(work_full, 1)

            steps = every_step | {
                "turn_in": lambda f, i: to_channels(f, 0), "in": dense("in", hT, modulated), "pool": pool,
                "out": dense("out", catT, lambda f: pe.wait_ge(cat_ready, f + 1)), "to_tokens": to_tokens,
                "turn_mid": lambda f, i: to_channels(f, 1), "to_h2": to_h2, "q": dense("q", hT, modulated_mid),
                "scores": score, "ada": ada}

            def summing(s, width):
                G0 = first_chunk(s)

                def body(c, r, n, first=False, last_one=False):
                    pe.wait_ge(diag_ready, c + (G0 + 1))
                    for j in range(KPC):
                        for half in range(2):
                            last = nc.tensor.matmul(acc[0:width, half * 512:(half + 1) * 512], diag[:, r, j, 0:width],
                                                    ring[:, r * KPC + j, D + half * 512:D + (half + 1) * 512],
                                                    start=(first and j == 0), stop=(last_one and j == KPC - 1))
                    last.then_inc(chunk_used, 1)
                return body

            def gate2(s, parts):
                m = mod[s // 2]
                pe.wait_ge(mod_ready, len(PARTS) * (s // 2 + 1))
                for half in range(2):
                    b = bank()
                    for c in range(4):
                        col = m[:, G2 + half * 4 + c, 0:1].broadcast_to([P, P]) if parts == P else m[:, G2 + half * 4 + c, 1:NC9]
                        last = nc.tensor.matmul(b[0:parts, c * P:(c + 1) * P], col, ident[:, :], start=True, stop=True)
                    last.then_inc(work_full, 1)

            pe.wait_ge(made, 12)
            pe.wait_ge(consts_in, 16 * 4)
            pe.wait_ge(silu_done, 1)
            for name, f, i in prologue():
                steps[name](f, i)
            accs = [0]
            for s in range(FRONTS):
                body = summing(s, P)
                if accs[0]:
                    pe.wait_ge(acc_free, accs[0])
                run_stage(pe, s, lambda c, r, n: body(c, r, n, first=True), body,
                          lambda c, r, n: body(c, r, n, last_one=True), steps, gate2)
                accs[0] += 1
                if s % 2:
                    body = summing(s, NS)
                    pe.wait_ge(acc_free, accs[0])
                    for c in range(SAMPLE_CHUNKS):
                        g = TILE_CHUNKS + c
                        if c == SAMPLE_CHUNKS - 1:
                            gate2(s, NS)
                        over_chunks(pe, s, g, g + 1, lambda *at, c=c: body(*at, first=(c == 0),
                                                                           last_one=(c == SAMPLE_CHUNKS - 1)))
                    accs[0] += 1


def kernel(x_prompt, x_sample, state_conv, state_pool, c_prompt, c_sample, w_ada, b_ada, w_in, conv_w, pool_w,
           pool_scale, w_out, ln1_g, ln1_b, w_q, sub_keys, u_experts, v_experts, ln2_g, ln2_b):
    import concourse.bacc as _bacc
    from concourse.bass_utils import run_bass_kernel_spmd as _run

    a = {k: np.asarray(v) for k, v in locals().items() if not k.startswith("_")}

    def blocks(w):
        n = w.shape[2] // BW
        return np.ascontiguousarray(w.reshape(DEPTH, DC, P, n, BW).transpose(0, 3, 2, 1, 4)).reshape(DEPTH, n, P, BK)

    def per_channel(v, lead):
        v = v.reshape(*lead, -1, P)
        return np.moveaxis(v, -1, 0)

    cond = per_channel(np.concatenate([a["c_prompt"], a["c_sample"]]), (NC9,))
    small = np.concatenate([
        per_channel(a["b_ada"], (DEPTH,)).reshape(P, -1),
        per_channel(a["conv_w"], (DEPTH, CONV_W)).transpose(0, 1, 3, 2).reshape(P, -1),
        per_channel(a["pool_scale"], (DEPTH,)).reshape(P, -1),
        cond.transpose(0, 2, 1).reshape(P, -1)], axis=1)

    def states(s, width):
        s = per_channel(s, s.shape[:3]).transpose(1, 0, 4, 2, 3)
        return np.ascontiguousarray(np.concatenate([s, np.zeros(s.shape[:4] + (1,), s.dtype)], axis=4))

    arrays = {
        "x": a["x_prompt"].reshape(SEQ, D), "xs": a["x_sample"].reshape(NS, D), "small": small,
        "w_ada": blocks(a["w_ada"]), "w_in": blocks(a["w_in"]), "w_out": blocks(a["w_out"]), "w_q": blocks(a["w_q"]),
        "keys": a["sub_keys"].reshape(DEPTH, HEADS // PG, 2 * PG, N_KEYS, P).transpose(0, 1, 4, 2, 3)
        .reshape(DEPTH, HEADS // PG, P, 2 * PG * N_KEYS),
        "pool_w": a["pool_w"].transpose(0, 2, 1, 3).reshape(DEPTH, P, CB * P),
        "ln1": np.concatenate([a["ln1_g"], a["ln1_b"]], axis=1), "ln2": np.concatenate([a["ln2_g"], a["ln2_b"]], axis=1),
        "conv_st": states(a["state_conv"], 3), "pool_st": states(a["state_pool"], 16),
        "uv": np.concatenate([a["u_experts"].reshape(-1, D), a["v_experts"].reshape(-1, D)], axis=1),
    }
    arrays = {f"in_{k}": np.ascontiguousarray(v) for k, v in arrays.items()}
    outs = {"y": (SEQ, D), "ys": (NS, D), "st_new": (DEPTH, P, ST_OUT)}

    nc = _bacc.Bacc("TRN2", target_bir_lowering=False, num_devices=1)
    ins = [nc.dram_tensor(k, v.shape, F32, kind="ExternalInput").ap() for k, v in arrays.items()]
    out = [nc.dram_tensor(f"out_{k}", v, F32, kind="ExternalOutput").ap() for k, v in outs.items()]
    bounce = nc.dram_tensor("bounce", (4, 2, NS, 2 * TOPK), U32, kind="Internal").ap()
    build_trunk(nc, *ins, *out, bounce)
    r = _run(nc, [arrays], core_ids=[0]).results[0]

    st = r["out_st_new"]

    def rows(part, *dims):
        v = part.reshape(DEPTH, P, CB, *dims)
        return np.moveaxis(v, (2, 1), (-2, -1)).reshape(DEPTH, *dims, CB * P)

    return (r["out_y"].reshape(1, SEQ, D), r["out_ys"].reshape(NS, 1, D),
            rows(st[:, :, O_CP:O_PP], 1, 2), rows(st[:, :, O_PP:O_CS], 1, HIST),
            rows(st[:, :, O_CS:O_PS], NS, 2), rows(st[:, :, O_PS:ST_OUT], NS, HIST))
```
